# Optimizing a Trainium2 kernel written in Bass

```python
import jax
import jax.numpy as jnp
from jax import lax
import numpy as np

D_MODEL = 1024
BATCH = 1
SEQ = 128
DEPTH = 1
DEC_BATCH = 1
DEC_SEQ = 1024
PAST_LEN = 128

GRID_W = 64
D_FOURIER = 512
N_FOURIER_GROUPS = 8
FOURIER_GROUP = D_FOURIER // N_FOURIER_GROUPS
D_RWKV = D_MODEL - D_FOURIER
HEAD_SIZE = 64
N_RWKV_HEADS = D_RWKV // HEAD_SIZE
DECAY_LORA = 64
ICLR_LORA = 64
GATE_LORA = 128
D_RWKV_IN = 3 * D_RWKV + 2 * DECAY_LORA + 2 * ICLR_LORA + GATE_LORA
D_IN = D_FOURIER + D_RWKV_IN
D_FF = 2816
N_MOD = 9
RMS_EPS = 1e-6
GN_EPS = 64e-5

kernel_name = 'hybrid_fnet_rwkv7_diffusion_step'

def _rmsnorm(x, g):
    xf = x.astype(jnp.float32)
    y = xf * lax.rsqrt(jnp.mean(xf * xf, axis=-1, keepdims=True) + RMS_EPS)
    return (y * g.astype(jnp.float32)).astype(x.dtype)

def _modulate(h, shift, scale):
    return h * (1 + scale[:, None, :]) + shift[:, None, :]

def _swiglu(h, w_gate, w_up, w_down):
    return (jax.nn.silu(h @ w_gate) * (h @ w_up)) @ w_down

def _shift(p, axis, offset):
    n = p.shape[axis]
    pad = [(0, 0)] * p.ndim
    if offset > 0:
        body = lax.slice_in_dim(p, 0, n - offset, axis=axis)
        pad[axis] = (offset, 0)
    else:
        body = lax.slice_in_dim(p, -offset, n, axis=axis)
        pad[axis] = (0, -offset)
    return jnp.pad(body, pad)

def _token_shift(z, grid):
    B, S, C = z.shape
    q = z.reshape(B, S, C // 4, 4)
    if grid:
        rows = S // GRID_W
        g = q.reshape(B, rows, GRID_W, C // 4, 4)
        parts = [_shift(g[..., 0], 2, 1), _shift(g[..., 1], 2, -1),
                 _shift(g[..., 2], 1, 1), _shift(g[..., 3], 1, -1)]
    else:
        parts = [_shift(q[..., 0], 1, 1), _shift(q[..., 1], 1, -1),
                 _shift(q[..., 2], 1, 1), _shift(q[..., 3], 1, -1)]
    return jnp.stack(parts, axis=-1).reshape(B, S, C)

def _wkv7_scan(r, decay, k, v, kk, a, s0, reverse):
    def step(state, inp):
        r_t, w_t, k_t, v_t, kk_t, a_t = inp
        sa = jnp.einsum('bhvk,bhk->bhv', state, -kk_t)
        state = (state * w_t[:, :, None, :]
                 + sa[..., None] * (kk_t * a_t)[:, :, None, :]
                 + v_t[..., None] * k_t[:, :, None, :])
        return state, jnp.einsum('bhvk,bhk->bhv', state, r_t)
    xs = tuple(jnp.moveaxis(t, 1, 0) for t in (r, decay, k, v, kk, a))
    s_final, ys = lax.scan(step, s0, xs, reverse=reverse)
    return jnp.moveaxis(ys, 0, 1), s_final

def _mixer(h, s0_f, s0_b, grid, w_in, mu, w0, w2, a0, a2, g2, k_k, k_a, r_k, ln_w, ln_b, w_out):
    B, S, _ = h.shape
    f32 = jnp.float32
    proj = h @ w_in
    u = proj[..., :D_FOURIER]
    z = proj[..., D_FOURIER:]
    z = (z + mu * (_token_shift(z, grid) - z)).astype(f32)

    uf = u.astype(f32).reshape(B, S, N_FOURIER_GROUPS, FOURIER_GROUP)
    y_four = jnp.fft.fft2(uf, axes=(1, 3), norm='ortho').real.reshape(B, S, D_FOURIER)

    o1, o2, o3 = D_RWKV, 2 * D_RWKV, 3 * D_RWKV
    o4 = o3 + 2 * DECAY_LORA
    o5 = o4 + 2 * ICLR_LORA
    r, k, v = z[..., :o1], z[..., o1:o2], z[..., o2:o3]
    wd = z[..., o3:o4].reshape(B, S, 2, DECAY_LORA)
    ad = z[..., o4:o5].reshape(B, S, 2, ICLR_LORA)
    gd = z[..., o5:]

    def heads(t):
        return t.reshape(B, S, N_RWKV_HEADS, HEAD_SIZE)

    kk = heads(k * k_k.astype(f32))
    kk = kk / jnp.maximum(jnp.linalg.norm(kk, axis=-1, keepdims=True), 1e-12)
    r_h, v_h = heads(r), heads(v)
    r_k_h = r_k.astype(f32).reshape(N_RWKV_HEADS, HEAD_SIZE)

    ys, bonuses, finals = [], [], []
    for d, s0 in enumerate((s0_f, s0_b)):
        w_raw = w0[d] + jnp.tanh(wd[:, :, d]) @ w2[d]
        decay = jnp.exp(-jnp.exp(-jax.nn.softplus(-w_raw) - 0.5))
        a = jax.nn.sigmoid(a0[d] + ad[:, :, d] @ a2[d])
        k_d = heads(k * (1 + (a - 1) * k_a))
        y_d, s_d = _wkv7_scan(r_h, heads(decay), k_d, v_h, kk, heads(a),
                              s0.astype(f32), reverse=(d == 1))
        ys.append(y_d)
        bonuses.append(jnp.sum(r_h * k_d * r_k_h, axis=-1, keepdims=True) * v_h)
        finals.append(s_d)
    y_sum = ys[0] + ys[1]
    mean = jnp.mean(y_sum, axis=-1, keepdims=True)
    var = jnp.mean(jnp.square(y_sum - mean), axis=-1, keepdims=True)
    y_gn = ((y_sum - mean) * lax.rsqrt(var + GN_EPS)).reshape(B, S, D_RWKV) * ln_w + ln_b
    gate = jax.nn.sigmoid(gd) @ g2
    y_rwkv = (y_gn + (bonuses[0] + bonuses[1]).reshape(B, S, D_RWKV)) * gate

    mixed = jnp.concatenate([y_four, y_rwkv], axis=-1).astype(h.dtype)
    return mixed @ w_out, finals[0], finals[1]

def _layer(x, mod, s0_f, s0_b, grid, norm_g, ffn_gate, ffn_up, ffn_down, mixer_params):
    sh1, sc1, g1, sh2, sc2, g2, sh3, sc3, g3 = jnp.split(mod, N_MOD, axis=-1)
    h = _modulate(_rmsnorm(x, norm_g[0]), sh1, sc1)
    x = x + 0.5 * g1[:, None, :] * _swiglu(h, ffn_gate[0], ffn_up[0], ffn_down[0])
    h = _modulate(_rmsnorm(x, norm_g[1]), sh2, sc2)
    mixed, s_f, s_b = _mixer(h, s0_f, s0_b, grid, *mixer_params)
    x = x + g2[:, None, :] * mixed
    h = _modulate(_rmsnorm(x, norm_g[2]), sh3, sc3)
    x = x + 0.5 * g3[:, None, :] * _swiglu(h, ffn_gate[1], ffn_up[1], ffn_down[1])
    return x, s_f, s_b

def setup_inputs(seed: int = 0) -> dict:
    key = jax.random.key(seed)
    ks = jax.random.split(key, 32)
    f32 = jnp.float32

    def nrm(k, shape, s):
        return jax.random.normal(k, shape, f32) * s

    def unif(k, shape, lo, hi):
        return jax.random.uniform(k, shape, f32, lo, hi)

    L = DEPTH
    st_shape = (DEC_BATCH, DEPTH, N_RWKV_HEADS, HEAD_SIZE, HEAD_SIZE)
    return {
        'x_prompt': nrm(ks[0], (BATCH, SEQ, D_MODEL), 1.0),
        'x_sample': nrm(ks[1], (DEC_BATCH, DEC_SEQ, D_MODEL), 1.0),
        'state_fwd': nrm(ks[2], st_shape, 0.5),
        'state_bwd': nrm(ks[3], st_shape, 0.5),
        'c': nrm(ks[4], (DEC_BATCH, D_MODEL), 1.0),
        'c_ctx': nrm(ks[5], (D_MODEL,), 1.0),
        'w_mod': nrm(ks[6], (L, D_MODEL, N_MOD * D_MODEL), 0.5 * D_MODEL ** -0.5),
        'b_mod': nrm(ks[7], (L, N_MOD * D_MODEL), 0.02),
        'norm_g': 1.0 + nrm(ks[8], (L, 3, D_MODEL), 0.05),
        'ffn_w_gate': nrm(ks[9], (L, 2, D_MODEL, D_FF), D_MODEL ** -0.5),
        'ffn_w_up': nrm(ks[10], (L, 2, D_MODEL, D_FF), D_MODEL ** -0.5),
        'ffn_w_down': nrm(ks[11], (L, 2, D_FF, D_MODEL), D_FF ** -0.5),
        'w_in': nrm(ks[12], (L, D_MODEL, D_IN), D_MODEL ** -0.5),
        'shift_mu': unif(ks[13], (L, D_RWKV_IN), 0.2, 0.8),
        'decay_w0': unif(ks[14], (L, 2, D_RWKV), -6.0, -1.0),
        'decay_w2': nrm(ks[15], (L, 2, DECAY_LORA, D_RWKV), 0.5 * DECAY_LORA ** -0.5),
        'iclr_a0': nrm(ks[16], (L, 2, D_RWKV), 0.1),
        'iclr_a2': nrm(ks[17], (L, 2, ICLR_LORA, D_RWKV), 0.5 * ICLR_LORA ** -0.5),
        'gate_g2': nrm(ks[18], (L, GATE_LORA, D_RWKV), GATE_LORA ** -0.5),
        'k_k': 0.85 + nrm(ks[19], (L, D_RWKV), 0.05),
        'k_a': 1.0 + nrm(ks[20], (L, D_RWKV), 0.05),
        'r_k': nrm(ks[21], (L, D_RWKV), 0.1),
        'ln_x_w': 1.0 + nrm(ks[22], (L, D_RWKV), 0.05),
        'ln_x_b': nrm(ks[23], (L, D_RWKV), 0.02),
        'w_out': nrm(ks[24], (L, D_MODEL, D_MODEL), D_MODEL ** -0.5),
        'final_norm': 1.0 + nrm(ks[25], (D_MODEL,), 0.05),
    }

def reference(x_prompt, x_sample, state_fwd, state_bwd, c, c_ctx, w_mod, b_mod, norm_g,
              ffn_w_gate, ffn_w_up, ffn_w_down, w_in, shift_mu, decay_w0, decay_w2,
              iclr_a0, iclr_a2, gate_g2, k_k, k_a, r_k, ln_x_w, ln_x_b, w_out, final_norm):
    xp, xs = x_prompt, x_sample
    bp = xp.shape[0]
    zero_state = jnp.zeros((bp, N_RWKV_HEADS, HEAD_SIZE, HEAD_SIZE), jnp.float32)
    new_f, new_b = [], []
    for l in range(DEPTH):
        mp = (w_in[l], shift_mu[l], decay_w0[l], decay_w2[l], iclr_a0[l], iclr_a2[l],
              gate_g2[l], k_k[l], k_a[l], r_k[l], ln_x_w[l], ln_x_b[l], w_out[l])
        mod_ctx = jnp.broadcast_to(jax.nn.silu(c_ctx) @ w_mod[l] + b_mod[l], (bp, N_MOD * D_MODEL))
        xp, s_f, s_b = _layer(xp, mod_ctx, zero_state, zero_state, False, norm_g[l],
                              ffn_w_gate[l], ffn_w_up[l], ffn_w_down[l], mp)
        new_f.append(s_f.astype(x_prompt.dtype))
        new_b.append(s_b.astype(x_prompt.dtype))
        mod_lat = jax.nn.silu(c) @ w_mod[l] + b_mod[l]
        xs, _, _ = _layer(xs, mod_lat, state_fwd[:, l], state_bwd[:, l], True, norm_g[l],
                          ffn_w_gate[l], ffn_w_up[l], ffn_w_down[l], mp)
    y_prompt = _rmsnorm(xp, final_norm)
    y_sample = _rmsnorm(xs, final_norm)
    return (y_prompt, y_sample, jnp.stack(new_f, axis=1), jnp.stack(new_b, axis=1))


_drawn_inputs = setup_inputs


def setup_inputs(seed=0):
    import zlib

    import numpy as np

    out = dict(_drawn_inputs(seed))
    spreads = {}
    factors = {'state_fwd': 8.0, 'state_bwd': 8.0, 'ln_x_w': 8.0, 'ln_x_b': 34.479}
    for name, (base, spread) in spreads.items():
        noise = np.random.default_rng([zlib.crc32(name.encode()), seed]).standard_normal(out[name].shape)
        drawn = base * np.exp(spread * noise) if base else spread * noise
        out[name] = jnp.asarray(drawn.astype(out[name].dtype))
    for name, factor in factors.items():
        out[name] = (out[name] * factor).astype(out[name].dtype)
    return out
```

```python
from contextlib import ExitStack

import numpy as np

import concourse.bass as bass
from concourse import mybir

ALU = mybir.AluOpType
ACT = mybir.ActivationFunctionType
F32 = mybir.dt.float32
F32R = mybir.dt.float32r
BF16 = mybir.dt.bfloat16

P = 128
D = 1024
KD = D // P
TS = 1024
TP = 128
T = TS + TP
NT = T // P
NC = 3
CW = T // NC
STREAMS = ((0, TS), (TS, T))
GRID_W = 64
FF = 2816
GROUPS = FF // P // 2
NMOD = 9
DH = 512
NP = DH // P
HS = 64
NCH = T // HS
SCH = TS // HS
NZ = 15
DECAY = float(np.exp(-0.5))
RMS_EPS = 1e-6
GN_EPS = 64e-5

PRM = {}
for _name, _n in (("c", 8), ("c_ctx", 8), ("norm_g", 24), ("final_norm", 8), ("shift_mu", 15), ("w0", 8), ("a0", 8),
                  ("k_k", 4), ("k_a", 4), ("r_k", 4), ("ln_w", 4), ("ln_b", 4)):
    PRM[_name] = sum(n for _, n in PRM.values()), _n
NPRM = sum(n for _, n in PRM.values())

C_ID, C_MASK, C_ONE, C_BLK, C_CLS = 0, 128, 384, 512, 640
NCST = 644


def constants():
    c = np.zeros((P, NCST), np.float32)
    c[:, C_ID:C_ID + P] = np.eye(P)
    s, t = np.arange(P)[:, None] % HS, np.arange(HS)[None, :]
    c[:, C_MASK:C_MASK + 256] = np.concatenate([s < t, s <= t, s > t, s >= t], 1)
    c[:, C_ONE:C_ONE + P] = 1.0 / D
    c[:, C_BLK:C_BLK + P] = np.kron(np.eye(2), np.ones((HS, HS)))
    c[:, C_CLS:C_CLS + 4] = np.arange(P)[:, None] % 4 == np.arange(4)[None, :]
    f = np.arange(HS)
    ang = 2 * np.pi * ((f[:, None] * f[None, :]) % HS) / HS
    feat = np.stack([np.concatenate([np.kron(np.eye(2), np.cos(ang)), np.kron(np.eye(2), -np.sin(ang))], 1)
                     / np.sqrt(n * HS) for n in (TS, TP)], 1)
    tabs = []
    for n in (TS, TP):
        i = np.arange(n, dtype=np.int64)
        a = 2 * np.pi * ((i[:, None] * i[None, :]) % n) / n
        tabs.append(np.stack([np.cos(a), np.sin(a)], 1).astype(np.float32))
    return c, feat.astype(np.float32), tabs[0], tabs[1]


class Steps:

    def __init__(self, sem, names):
        self.sem, self.names, self.n = sem, list(names), 0
        self.count = {name: i + 1 for i, name in enumerate(self.names)}
        assert len(self.count) == len(self.names)

    def did(self, name, ins):
        assert self.names[self.n] == name, (self.names[self.n], name)
        self.n += 1
        ins.then_inc(self.sem, 1)

    def wait(self, eng, name):
        eng.wait_ge(self.sem, self.count[name])


class Stage:

    def __init__(self, nc):
        self.nc, self.sems, self.ctx = nc, [], ExitStack()

    def sem(self, name):
        s = self.ctx.enter_context(self.nc.semaphore(name))
        self.sems.append(s)
        return s

    def __enter__(self):
        self.ctx.__enter__()
        return self

    def block(self):
        return self.nc.Block()

    def __exit__(self, *a):
        if a[0] is None:
            with self.nc.Block() as block:
                @block.sync
                def _(sp):
                    for s in self.sems:
                        sp.sem_clear(s)
        return self.ctx.__exit__(*a)


def mm3(pe, out, w_hi, w_lo, x_hi, x_lo, start, stop):
    pe.matmul(out, w_lo, x_hi, start=start, stop=False)
    pe.matmul(out, w_hi, x_lo, start=False, stop=False)
    return pe.matmul(out, w_hi, x_hi, start=False, stop=stop)


def parts(c):
    out = []
    for s, (a, b) in enumerate(STREAMS):
        lo, hi = max(a, c * CW), min(b, (c + 1) * CW)
        if lo < hi:
            out.append((s, lo - c * CW, hi - c * CW))
    return out


def load_stage(nc, io, sb):
    with Stage(nc) as st, nc.psum_tensor("ld_ps", [P, 8, 512], F32) as ps, \
            nc.sbuf_tensor("ld_x", [P, NT, D], F32) as xin, nc.sbuf_tensor("ld_p", [P, 2, P], F32) as prow:
        consts_in, rows_in = st.sem("consts_in"), st.sem("rows_in")
        x_in = [st.sem(f"x_in{t}") for t in range(NT)]
        pe_s, dve_s, act_s = st.sem("pe_s"), st.sem("dve_s"), st.sem("act_s")
        pe_t = Steps(pe_s, ["prm", "bias"] + [f"x{n}" for n in range(2 * NT)])
        dve_t = Steps(dve_s, ["prm", "bias"] + [f"x{n}" for n in range(0, 2 * NT, 2)])
        act_t = Steps(act_s, [f"x{n}" for n in range(1, 2 * NT, 2)])
        rows = [(io["c"], "c"), (io["c_ctx"].rearrange("(a n) -> a n", a=1), "c_ctx"),
                (io["norm_g"].rearrange("l i n -> (l i) n"), "norm_g"),
                (io["final_norm"].rearrange("(a n) -> a n", a=1), "final_norm"), (io["shift_mu"], "shift_mu"),
                (io["decay_w0"].rearrange("l i n -> (l i) n"), "w0"), (io["iclr_a0"].rearrange("l i n -> (l i) n"), "a0"),
                (io["k_k"], "k_k"), (io["k_a"], "k_a"), (io["r_k"], "r_k"), (io["ln_x_w"], "ln_w"), (io["ln_x_b"], "ln_b")]
        with st.block() as block:
            @block.sync
            def _(sp):
                sp.dma_start(sb["cst"][:, :], io["consts"]).then_inc(consts_in, 16)
                for t in range(0, NT):
                    src = io["x_sample"][0, t * P:(t + 1) * P, :] if t * P < TS else io["x_prompt"][0, :, :]
                    sp.dma_start(xin[:, t, :], src).then_inc(x_in[t], 16)

            @block.scalar
            def _(act):
                for src, name in rows:
                    at, n = PRM[name]
                    act.dma_start(prow[at:at + n, 0, :], src.rearrange("i (k p) -> (i k) p", p=P)).then_inc(rows_in, 16)
                act.dma_start(prow[0:NMOD * KD, 1, :], io["b_mod"].rearrange("i (k p) -> (i k) p", p=P))\
                   .then_inc(rows_in, 16)
                for n in range(1, 2 * NT, 2):
                    t, half = n // 2, n % 2
                    pe_t.wait(act, f"x{n}")
                    act_t.did(f"x{n}", act.activation(
                        sb["x"][:, half * 4:half * 4 + 4, t * P:(t + 1) * P],
                        ps[:, n % 6, :].rearrange("p (k t) -> p k t", k=4), ACT.Copy))

            @block.tensor
            def _(pe):
                pe.wait_ge(consts_in, 16)
                pe.wait_ge(rows_in, 16 * (len(rows) + 1))
                ident = sb["cst"][:, C_ID:C_ID + P]
                pe_t.did("prm", pe.transpose(ps[:, 6, 0:NPRM], prow[0:NPRM, 0, :], ident[0:NPRM, 0:NPRM]))
                nb = NMOD * KD
                pe_t.did("bias", pe.transpose(ps[:, 7, 0:nb], prow[0:nb, 1, :], ident[0:nb, 0:nb]))
                for n in range(2 * NT):
                    t, half = n // 2, n % 2
                    if half == 0:
                        pe.wait_ge(x_in[t], 16)
                    if n >= 6:
                        (dve_t if n % 2 == 0 else act_t).wait(pe, f"x{n - 6}")
                    for k in range(4):
                        last = pe.transpose(ps[:, n % 6, k * P:(k + 1) * P],
                                            xin[:, t, (half * 4 + k) * P:(half * 4 + k + 1) * P], ident)
                    pe_t.did(f"x{n}", last)

            @block.vector
            def _(dve):
                pe_t.wait(dve, "prm")
                dve_t.did("prm", dve.tensor_copy(sb["prm"][:, :], ps[:, 6, 0:NPRM]))
                pe_t.wait(dve, "bias")
                dve_t.did("bias", dve.tensor_copy(sb["bmod"][:, :], ps[:, 7, 0:NMOD * KD]))
                for n in range(0, 2 * NT, 2):
                    t, half = n // 2, n % 2
                    pe_t.wait(dve, f"x{n}")
                    dve_t.did(f"x{n}", dve.tensor_copy(
                        sb["x"][:, half * 4:half * 4 + 4, t * P:(t + 1) * P],
                        ps[:, n % 6, :].rearrange("p (k t) -> p k t", k=4)))


def mod_stage(nc, io, sb):
    SLOTS = 3
    with Stage(nc) as st, nc.psum_tensor("md_ps", [P, 4, 512], F32) as ps, \
            nc.sbuf_tensor("md_w", [P, SLOTS, KD, D], F32) as w, nc.sbuf_tensor("md_c", [P, KD, 32], F32) as cpad, \
            nc.sbuf_tensor("md_sum", [P, 2, 512], F32) as sums, nc.sbuf_tensor("md_q", [P, 2, 16], F32) as quad:
        w_in = [st.sem(f"w_in{n}") for n in range(SLOTS)]
        c_zero, c_ready, summed, copied = st.sem("c_zero"), st.sem("c_ready"), st.sem("summed"), st.sem("copied")
        turned, quad_copied, own, done = st.sem("turned"), st.sem("quad_copied"), st.sem("own"), st.sem("done")
        wsrc = io["w_mod"].rearrange("l (k p) n -> p (l k) n", p=P)
        with st.block() as block:
            @block.sync
            def _(sp):
                for j in range(SLOTS):
                    sp.dma_start(w[:, j, :, :], wsrc[:, :, j * D:(j + 1) * D]).then_inc(w_in[j], 16)
                with sp.Fori(0, NMOD // SLOTS - 1) as i:
                    for j in range(SLOTS):
                        sp.wait_ge(summed, i * SLOTS + (j + 1))
                        sp.dma_start(w[:, j, :, :], wsrc[:, :, bass.ds(i * (SLOTS * D) + (SLOTS + j) * D, D)])\
                          .then_inc(w_in[j], 16)

            @block.gpsimd
            def _(pool):
                pool.memset(cpad[:, :, :], 0.0).then_inc(c_zero, 1)

            @block.scalar
            def _(act):
                act.wait_ge(c_zero, 1)
                for s, name in enumerate(("c", "c_ctx")):
                    at, n = PRM[name]
                    act.activation(cpad[:, :, s:s + 1], sb["prm"][:, at:at + n].unsqueeze(2), ACT.Silu)\
                       .then_inc(c_ready, 1)

            @block.tensor
            def _(pe):
                pe.wait_ge(c_ready, 2)
                ident = sb["cst"][:, C_ID:C_ID + P]
                with pe.Fori(0, NMOD // SLOTS) as i:
                    for j in range(SLOTS):
                        pe.wait_ge(w_in[j], i * 16 + 16)
                        for kk in range(KD // 2):
                            for g in range(4):
                                n, k = g // 2, g % 2 * (KD // 2) + kk
                                last = pe.matmul(ps[32 * g:32 * g + 32, 0, :], cpad[:, k, :],
                                                 w[:, j, k, n * 512:(n + 1) * 512], start=kk == 0, stop=kk == KD // 2 - 1)
                        last.then_inc(summed, 1)
                        pe.wait_ge(copied, i * SLOTS + (j + 1))
                        pe.wait_ge(quad_copied, i * SLOTS + (j + 1))
                        for cc in range(4):
                            last = pe.transpose(ps[:, 1, cc * P:(cc + 1) * P], sums[:, 0, cc * P:(cc + 1) * P], ident)
                        last.then_inc(turned, 1)

            @block.vector
            def _(dve):
                dve.sem_inc(quad_copied, 1)
                with dve.Fori(0, NMOD // SLOTS) as i:
                    for j in range(SLOTS):
                        dve.wait_ge(summed, i * SLOTS + (j + 1))
                        dve.tensor_copy(sums[:, 0, :], ps[:, 0, :]).then_inc(copied, 1)
                        dve.wait_ge(turned, i * SLOTS + (j + 1))
                        for n in range(2):
                            for kh in range(2):
                                c0 = 64 * n + 32 * kh
                                last = dve.tensor_copy(
                                    quad[:, kh, 8 * n:8 * n + 8].rearrange("p (c s) -> p c s", s=2),
                                    ps[:, 1, :].rearrange("p (c q) -> p c q", q=P)[:, :, c0:c0 + 2])
                                last.then_inc(own, 1)
                        dve.wait_ge(own, i * (4 * SLOTS) + 4 * (j + 1))
                        dve.tensor_tensor(sb["mod"][:, bass.ds(i * (SLOTS * KD) + j * KD, KD), :],
                                          quad[:, 0, :].rearrange("p (c s) -> p c s", s=2),
                                          quad[:, 1, :].rearrange("p (c s) -> p c s", s=2), ALU.add)\
                           .then_inc(quad_copied, 1)
                        dve.wait_ge(quad_copied, i * SLOTS + (j + 2))
                mod = sb["mod"]
                steps = Steps(done, ["bias", "sc", "g", "h0", "h2"])
                steps.did("bias", dve.tensor_tensor(mod[:, :, :], mod[:, :, :],
                                                    sb["bmod"][:, :].unsqueeze(2).to_broadcast([P, NMOD * KD, 2]), ALU.add))
                steps.wait(dve, "bias")
                mv = mod[:, :, :].rearrange("p (i m k) s -> p i m (k s)", i=3, m=3)
                at, n = PRM["norm_g"]
                steps.did("sc", dve.tensor_scalar(mv[:, :, 1, :], mv[:, :, 1, :], 1.0, None, ALU.add))
                steps.wait(dve, "sc")
                for i in range(3):
                    m = mod[:, (3 * i + 1) * KD:(3 * i + 2) * KD, :]
                    last = dve.tensor_tensor(m, m, sb["prm"][:, at + i * KD:at + (i + 1) * KD].unsqueeze(2)
                                             .to_broadcast([P, KD, 2]), ALU.mult)
                steps.did("g", last)
                steps.did("h0", dve.tensor_scalar(mv[:, 0, 2, :], mv[:, 0, 2, :], 0.5, None, ALU.mult))
                steps.did("h2", dve.tensor_scalar(mv[:, 2, 2, :], mv[:, 2, 2, :], 0.5, None, ALU.mult))


def norm_stage(nc, sb, i, h_hi, h_lo):
    final = h_lo is None
    with Stage(nc) as st, nc.psum_tensor(f"nm_ps{i}", [P, 4, 512], F32) as ps, \
            nc.sbuf_tensor(f"nm_sq{i}", [P, 2, T], F32) as sq, nc.sbuf_tensor(f"nm_r{i}", [P, T], F32) as rstd:
        x = sb["x"]
        pe_t = Steps(st.sem("pe_s"), [f"sum{k}" for k in range(KD)])
        act_t = Steps(st.sem("act_s"), [f"sq{k}" for k in range(KD)] + ["sqrt"] + [f"hi{k}" for k in range(KD * (not final))])
        dve_t = Steps(st.sem("dve_s"), ["ms", "rstd"] + [f"{a}{k}" for k in range(KD) for a in (("n",) if final else ("n", "lo"))])

        def scale(k, s):
            if final:
                return sb["prm"][:, PRM["final_norm"][0] + k:PRM["final_norm"][0] + k + 1]
            return sb["mod"][:, (3 * i + 1) * KD + k, s:s + 1]

        def shift(k, s):
            return sb["mod"][:, 3 * i * KD + k, s:s + 1]

        with st.block() as block:
            @block.scalar
            def _(act):
                for k in range(KD):
                    if k >= 2:
                        pe_t.wait(act, f"sum{k - 2}")
                    act_t.did(f"sq{k}", act.activation(sq[:, k % 2, :], x[:, k, :], ACT.Square))
                dve_t.wait(act, "ms")
                act_t.did("sqrt", act.activation(rstd[:, :], rstd[:, :], ACT.Sqrt))
                if not final:
                    for k in range(KD):
                        dve_t.wait(act, f"n{k}")
                        for s, (a, b) in enumerate(STREAMS):
                            last = act.activation(h_hi[:, k, a:b], sq[:, k % 2, a:b], ACT.Identity, bias=shift(k, s))
                        act_t.did(f"hi{k}", last)

            @block.tensor
            def _(pe):
                for k in range(KD):
                    act_t.wait(pe, f"sq{k}")
                    for c in range(NC):
                        last = pe.matmul(ps[:, c, 0:CW], sb["cst"][:, C_ONE:C_ONE + P], sq[:, k % 2, c * CW:(c + 1) * CW],
                                         start=k == 0, stop=k == KD - 1)
                    pe_t.did(f"sum{k}", last)

            @block.vector
            def _(dve):
                pe_t.wait(dve, f"sum{KD - 1}")
                dve_t.did("ms", dve.tensor_scalar(rstd[:, :].rearrange("p (c n) -> p c n", c=NC), ps[:, 0:NC, 0:CW],
                                                  RMS_EPS, None, ALU.add))
                act_t.wait(dve, "sqrt")
                dve_t.did("rstd", dve.reciprocal(rstd[:, :], rstd[:, :]))
                dve_t.wait(dve, "rstd")
                for k in range(KD):
                    if final:
                        last = dve.scalar_tensor_tensor(h_hi[:, k, :], x[:, k, :], scale(k, 0), rstd[:, :], ALU.mult, ALU.mult)
                        dve_t.did(f"n{k}", last)
                        continue
                    for s, (a, b) in enumerate(STREAMS):
                        last = dve.scalar_tensor_tensor(sq[:, k % 2, a:b], x[:, k, a:b], scale(k, s), rstd[:, a:b],
                                                        ALU.mult, ALU.mult)
                    dve_t.did(f"n{k}", last)
                    act_t.wait(dve, f"hi{k}")
                    for s, (a, b) in enumerate(STREAMS):
                        last = dve.scalar_tensor_tensor(h_lo[:, k, a:b], sq[:, k % 2, a:b], shift(k, s),
                                                        h_hi[:, k, a:b].bitcast(F32), ALU.add, ALU.subtract)
                    dve_t.did(f"lo{k}", last)


def ffn_stage(nc, io, sb, f, h_hi, h_lo):
    UNITS, RAW = 6, 3
    G0, U0, G1, U1, D0, D1 = range(UNITS)
    x = sb["x"]
    with Stage(nc) as st, nc.psum_tensor(f"ff_ps{f}", [P, 8, 512], F32) as ps, \
            nc.sbuf_tensor(f"ff_raw{f}", [P, RAW, D], F32) as raw, nc.sbuf_tensor(f"ff_whi{f}", [P, UNITS, D], F32R) as w_hi, \
            nc.sbuf_tensor(f"ff_wlo{f}", [P, UNITS, D], F32R) as w_lo, \
            nc.sbuf_tensor(f"ff_s{f}", [P, 2, CW], F32) as silu, nc.sbuf_tensor(f"ff_u{f}", [P, 2, CW], F32) as hid, \
            nc.sbuf_tensor(f"ff_uhi{f}", [P, 2, T], F32R) as hid_hi, nc.sbuf_tensor(f"ff_ulo{f}", [P, 2, T], F32R) as hid_lo:
        raw_in = [st.sem(f"raw_in{n}") for n in range(RAW)]
        w_hi_s, w_lo_s = st.sem("w_hi_s"), st.sem("w_lo_s")
        gate_done, up_done, down_done = st.sem("gate_done"), st.sem("up_done"), st.sem("down_done")
        gate_free, up_free, down_free = st.sem("gate_free"), st.sem("up_free"), st.sem("down_free")
        hid_hi_s, hid_lo_s = st.sem("hid_hi_s"), st.sem("hid_lo_s")
        TILES, DOWNS = 2 * NC, NC * KD

        def unit_src(g, u):
            if u in (D0, D1):
                return io["ffn_w_down"][0, f, bass.ds((g * 2 + (u - D0)) * P, P), :]
            src = io["ffn_w_gate"] if u in (G0, G1) else io["ffn_w_up"]
            m = u // 2
            return src[0, f].rearrange("(k p) n -> p k n", p=P)[:, :, bass.ds((g * 2 + m) * P, P)]

        def unit_dst(t, u, slot):
            return t[:, slot, :] if u in (D0, D1) else t[:, slot, :].rearrange("p (k n) -> p k n", k=KD)

        with st.block() as block:
            @block.sync
            def _(sp):
                for u in range(RAW):
                    sp.dma_start(unit_dst(raw, u, u), unit_src(0, u)).then_inc(raw_in[u], 16)

                def rest(g):
                    for u in range(RAW, UNITS):
                        sp.wait_ge(w_lo_s, g * UNITS + (u - RAW + 1))
                        sp.dma_start(unit_dst(raw, u, u % RAW), unit_src(g, u)).then_inc(raw_in[u % RAW], 16)

                with sp.Fori(0, GROUPS - 1) as g:
                    rest(g)
                    for u in range(RAW):
                        sp.wait_ge(w_lo_s, g * UNITS + (u + RAW + 1))
                        sp.dma_start(unit_dst(raw, u, u), unit_src(g + 1, u)).then_inc(raw_in[u], 16)
                rest(GROUPS - 1)

            @block.tensor
            def _(pe):
                def group(g):
                    for t in range(TILES):
                        m, c = t // NC, t % NC
                        cols = slice(c * CW, (c + 1) * CW)
                        for which, base, free, done in ((G0, 0, gate_free, gate_done), (U0, 2, up_free, up_done)):
                            u = which + 2 * m
                            if c == 0:
                                pe.wait_ge(w_lo_s, g * UNITS + (u + 1))
                            pe.wait_ge(free, g * TILES + (t + 1))
                            for k in range(KD):
                                ks = slice(k * P, (k + 1) * P)
                                last = mm3(pe, ps[:, base + t % 2, 0:CW], w_hi[:, u, ks], w_lo[:, u, ks],
                                           h_hi[:, k, cols], h_lo[:, k, cols], k == 0, k == KD - 1)
                            last.then_inc(done, 1)
                    for n in range(DOWNS):
                        c, o = n // KD, n % KD
                        if n == 0:
                            pe.wait_ge(w_lo_s, g * UNITS + UNITS)
                        if o == 0:
                            pe.wait_ge(hid_lo_s, g * TILES + (NC + c + 1))
                        pe.wait_ge(down_free, g * DOWNS + (n + 1))
                        for m in range(2):
                            os = slice(o * P, (o + 1) * P)
                            cols = slice(c * CW, (c + 1) * CW)
                            last = mm3(pe, ps[:, 4 + n % 4, 0:CW], w_hi[:, D0 + m, os], w_lo[:, D0 + m, os],
                                       hid_hi[:, m, cols], hid_lo[:, m, cols], m == 0, m == 1)
                        last.then_inc(down_done, 1)
                with pe.Fori(0, GROUPS - 1) as g:
                    group(g)
                group(GROUPS - 1)

            @block.scalar
            def _(act):
                act.sem_inc(gate_free, 2)

                def split(g, u):
                    act.wait_ge(raw_in[u % RAW], (g * 2 + (u // RAW + 1)) * 16)
                    act.activation(w_hi[:, u, :], raw[:, u % RAW, :], ACT.Copy).then_inc(w_hi_s, 1)

                def hidden(g, t):
                    act.wait_ge(gate_done, g * TILES + (t + 1))
                    act.wait_ge(up_free, g * TILES + (t + 1))
                    act.activation(silu[:, t % 2, :], ps[:, t % 2, 0:CW], ACT.Silu).then_inc(gate_free, 1)
                    m, c = t // NC, t % NC
                    act.wait_ge(up_free, g * TILES + (t + 3))
                    act.wait_ge(down_free, g * DOWNS + 4)
                    act.activation(hid_hi[:, m, c * CW:(c + 1) * CW], hid[:, t % 2, :], ACT.Copy).then_inc(hid_hi_s, 1)

                def group(g, last):
                    for m in range(2):
                        for c in range(NC):
                            hidden(g, m * NC + c)
                        if not last:
                            act.wait_ge(up_done, g * TILES + NC * (m + 1))
                            split(g + 1, G0 + 2 * m)
                            split(g + 1, U0 + 2 * m)
                    if not last:
                        act.wait_ge(down_done, g * DOWNS + DOWNS)
                        split(g + 1, D0)
                        split(g + 1, D1)

                for u in range(UNITS):
                    split(0, u)
                with act.Fori(0, GROUPS - 1) as g:
                    group(g, False)
                group(GROUPS - 1, True)

            @block.vector
            def _(dve):
                dve.sem_inc(up_free, 2)
                dve.sem_inc(down_free, 4)

                def split(g, u):
                    dve.wait_ge(w_hi_s, g * UNITS + (u + 1))
                    dve.tensor_tensor(w_lo[:, u, :], raw[:, u % RAW, :], w_hi[:, u, :].bitcast(F32), ALU.subtract)\
                       .then_inc(w_lo_s, 1)

                def hidden(g, t):
                    m, c = t // NC, t % NC
                    dve.wait_ge(gate_free, g * TILES + (t + 3))
                    dve.wait_ge(up_done, g * TILES + (t + 1))
                    dve.tensor_tensor(hid[:, t % 2, :], ps[:, 2 + t % 2, 0:CW], silu[:, t % 2, :], ALU.mult)\
                       .then_inc(up_free, 1)
                    dve.wait_ge(hid_hi_s, g * TILES + (t + 1))
                    dve.tensor_tensor(hid_lo[:, m, c * CW:(c + 1) * CW], hid[:, t % 2, :],
                                      hid_hi[:, m, c * CW:(c + 1) * CW].bitcast(F32), ALU.subtract).then_inc(hid_lo_s, 1)

                def update(g, n):
                    c, o = n // KD, n % KD
                    dve.wait_ge(down_done, g * DOWNS + (n + 1))
                    for s, a, b in parts(c):
                        xs = x[:, o, c * CW + a:c * CW + b]
                        last = dve.scalar_tensor_tensor(xs, ps[:, 4 + n % 4, a:b],
                                                        sb["mod"][:, (3 * (2 * f) + 2) * KD + o, s:s + 1], xs,
                                                        ALU.mult, ALU.add)
                    last.then_inc(down_free, 1)

                def group(g, last):
                    for m in range(2):
                        for c in range(NC):
                            hidden(g, m * NC + c)
                        if not last:
                            split(g + 1, G0 + 2 * m)
                            split(g + 1, U0 + 2 * m)
                    for n in range(DOWNS):
                        update(g, n)
                    if not last:
                        split(g + 1, D0)
                        split(g + 1, D1)

                for u in range(UNITS):
                    split(0, u)
                with dve.Fori(0, GROUPS - 1) as g:
                    group(g, False)
                group(GROUPS - 1, True)


def project_stage(nc, io, sb, h_hi, h_lo, zd, u):
    RAW = 2
    with Stage(nc) as st, nc.psum_tensor("pj_ps", [P, 8, 512], F32) as ps, \
            nc.sbuf_tensor("pj_raw", [P, RAW, D], F32) as raw, nc.sbuf_tensor("pj_whi", [P, 2, D], F32R) as w_hi, \
            nc.sbuf_tensor("pj_wlo", [P, 2, D], F32R) as w_lo, nc.sbuf_tensor("pj_z", [P, 2, T], F32) as z, \
            nc.sbuf_tensor("pj_zo", [P, 2, T], F32) as zo, nc.sbuf_tensor("pj_mu", [P, NZ, 7], F32) as mu:
        raw_in = [st.sem(f"raw_in{n}") for n in range(RAW)]
        z_out = [st.sem(f"z_out{n}") for n in range(2)]
        w_hi_s, w_lo_s, chunk_done, chunk_free = st.sem("w_hi_s"), st.sem("w_lo_s"), st.sem("chunk_done"), st.sem("chunk_free")
        z_copied, shifted, own, mu_s, z_free = st.sem("z_copied"), st.sem("shifted"), st.sem("own"), st.sem("mu_s"), st.sem("z_free")
        wsrc = io["w_in"][0].rearrange("(k p) n -> p k n", p=P)
        NU = NP
        PAIRS, LAST = NZ // 2, NZ - 1
        ADDS = 6
        TILES = NZ + NU

        def load(sp, i, slot):
            col = (i + NU) * P if not isinstance(i, int) or i < NZ else (i - NZ) * P
            sp.dma_start(raw[:, slot, :].rearrange("p (k n) -> p k n", k=KD), wsrc[:, :, bass.ds(col, P)])\
              .then_inc(raw_in[slot], 16)

        with st.block() as block:
            @block.sync
            def _(sp):
                def store(i, b):
                    sp.wait_ge(shifted, i + 1)
                    dst = zd[bass.ds(i, 1), :, :].rearrange("a p t -> p (a t)")
                    sp.dma_start(dst, zo[:, b, :]).then_inc(z_out[b], 16)

                for n in range(4):
                    if n >= 2:
                        sp.wait_ge(w_lo_s, n - 1)
                    load(sp, n, n % 2)
                AHEAD = (NZ - 4) // 2
                with sp.Fori(0, AHEAD) as i:
                    for b in range(2):
                        store(i * 2 + b, b)
                        sp.wait_ge(w_lo_s, i * 2 + (b + 3))
                        load(sp, i * 2 + (b + 4), b)
                for n in range(2 * AHEAD, NZ):
                    store(n, n % 2)
                    if n + 4 < TILES:
                        sp.wait_ge(w_lo_s, n + 3)
                        load(sp, n + 4, n % 2)
                sp.wait_ge(z_out[0], 16 * (PAIRS + 1))
                sp.wait_ge(z_out[1], 16 * PAIRS)

            @block.tensor
            def _(pe):
                def tile(i, b):
                    pe.wait_ge(w_lo_s, i + 1)
                    for c in range(NC):
                        cols = slice(c * CW, (c + 1) * CW)
                        pe.wait_ge(chunk_free, i * NC + (c + 1))
                        for k in range(KD):
                            ks = slice(k * P, (k + 1) * P)
                            last = mm3(pe, ps[:, 4 * b + c, 0:CW], w_hi[:, b, ks], w_lo[:, b, ks],
                                       h_hi[:, k, cols], h_lo[:, k, cols], k == 0, k == KD - 1)
                        last.then_inc(chunk_done, 1)
                with pe.Fori(0, PAIRS) as i:
                    for b in range(2):
                        tile(i * 2 + b, b)
                for n in range(2 * PAIRS, TILES):
                    tile(n, n % 2)

            @block.scalar
            def _(act):
                act.sem_inc(chunk_free, 2 * NC)

                def z_tile(i, b):
                    act.wait_ge(z_free, i + 1)
                    for c in range(NC):
                        act.wait_ge(chunk_done, i * NC + (c + 1))
                        act.activation(z[:, b, c * CW:(c + 1) * CW], ps[:, 4 * b + c, 0:CW], ACT.Copy).then_inc(chunk_free, 1)

                def upper(i, b, count):
                    act.wait_ge(raw_in[b], count)
                    act.activation(w_hi[:, b, :], raw[:, b, :], ACT.Copy).then_inc(w_hi_s, 1)

                upper(0, 0, 16)
                upper(1, 1, 16)
                with act.Fori(0, PAIRS) as i:
                    for b in range(2):
                        z_tile(i * 2 + b, b)
                        upper(i * 2 + b + 2, b, (i + 2) * 16)
                for n in range(2 * PAIRS, TILES):
                    if n < NZ:
                        z_tile(n, n % 2)
                    else:
                        for c in range(NC):
                            act.wait_ge(chunk_done, n * NC + c + 1)
                            act.activation(u[:, n - NZ, c * CW:(c + 1) * CW], ps[:, 4 * (n % 2) + c, 0:CW], ACT.Copy)\
                               .then_inc(chunk_free, 1)
                    if n + 2 < TILES:
                        upper(n + 2, n % 2, 16 * ((n + 2) // 2 + 1))

            @block.vector
            def _(dve):
                dve.sem_inc(z_free, 2)
                at, _n = PRM["shift_mu"]
                muv, cls = sb["prm"][:, at:at + NZ], sb["cst"][:, C_CLS:C_CLS + 4]
                mt = Steps(mu_s, ["m0", "m1", "m2", "m3", "one", "up", "down"])
                for j in range(4):
                    mt.did(f"m{j}", dve.tensor_scalar(mu[:, :, j], muv, cls[:, j:j + 1], None, ALU.mult))
                mt.did("one", dve.tensor_scalar(mu[:, :, 6], muv, -1.0, 1.0, ALU.mult, ALU.add))
                mt.wait(dve, "one")
                mt.did("up", dve.tensor_tensor(mu[:, :, 4], mu[:, :, 0], mu[:, :, 2], ALU.add))
                mt.did("down", dve.tensor_tensor(mu[:, :, 5], mu[:, :, 1], mu[:, :, 3], ALU.add))
                mt.wait(dve, "down")

                def lower(i, b):
                    dve.wait_ge(w_hi_s, i + 1)
                    dve.tensor_tensor(w_lo[:, b, :], raw[:, b, :], w_hi[:, b, :].bitcast(F32), ALU.subtract).then_inc(w_lo_s, 1)

                def z_tile(i, b, stored):
                    m = mu[:, bass.ds(i, 1), :].rearrange("p a j -> p (a j)")
                    dve.wait_ge(chunk_free, i * NC + 3 * NC)
                    if stored is not None:
                        dve.wait_ge(z_out[b], stored)
                    adds = []
                    zs, os = z[:, b, 0:TS], zo[:, b, 0:TS]
                    zg, og = (v.rearrange("p (r w) -> p r w", w=GRID_W) for v in (zs, os))
                    zp, op = z[:, b, TS:T], zo[:, b, TS:T]
                    adds = [(og[:, :, 1:], zg[:, :, :-1], 0), (op[:, 1:], zp[:, :-1], 4),
                            (og[:, :, :-1], zg[:, :, 1:], 1), (op[:, :-1], zp[:, 1:], 5),
                            (os[:, GRID_W:], zs[:, :-GRID_W], 2), (os[:, :-GRID_W], zs[:, GRID_W:], 3)]
                    dve.tensor_scalar(zo[:, b, :], z[:, b, :], m[:, 6:7], None, ALU.mult).then_inc(own, 1)
                    for n, (dst, src, j) in enumerate(adds):
                        dve.wait_ge(own, i * ADDS + (n + 1))
                        ins = dve.scalar_tensor_tensor(dst, src, m[:, j:j + 1], dst, ALU.mult, ALU.add)
                        if n < ADDS - 1:
                            ins.then_inc(own, 1)
                        else:
                            ins.then_inc(shifted, 1)
                    dve.wait_ge(shifted, i + 1)
                    dve.sem_inc(z_free, 1)

                lower(0, 0)
                lower(1, 1)
                for b in range(2):
                    z_tile(b, b, None)
                    lower(b + 2, b)
                with dve.Fori(1, PAIRS) as i:
                    for b in range(2):
                        z_tile(i * 2 + b, b, i * 16)
                        lower(i * 2 + (b + 2), b)
                z_tile(LAST, LAST % 2, 16 * PAIRS)
                for n in range(2 * PAIRS + 2, TILES):
                    lower(n, n % 2)


def fourier_stage(nc, io, sb, u, md):
    with Stage(nc) as st, nc.psum_tensor("fo_ps", [P, 8, 512], F32) as ps, \
            nc.sbuf_tensor("fo_f", [P, 2, 256], F32) as feat, nc.sbuf_tensor("fo_t", [P, NT, NP, 256], F32) as f, \
            nc.sbuf_tensor("fo_tab", [P, 2, 2, TS], F32) as tab, nc.sbuf_tensor("fo_tabp", [P, 2, TP], F32) as tabp, \
            nc.sbuf_tensor("fo_y", [P, NP, T], F32) as y:
        feat_in, tabp_in, y_out = st.sem("feat_in"), st.sem("tabp_in"), st.sem("y_out")
        tab_in = [st.sem("tab_in0"), st.sem("tab_in1")]
        pe_t = Steps(st.sem("pe_s"), [f"f{n}" for n in range(NT * 2)] + ["prompt"] + [f"t{t}" for t in range(SCH // 2)])
        copied = {0: st.sem("copied_dve"), 1: st.sem("copied_act")}
        y_s, p_free = st.sem("y_s"), st.sem("p_free")
        src = io["dft_s"].rearrange("(t p) a n -> p t a n", p=P)
        with st.block() as block:
            @block.sync
            def _(sp):
                sp.dma_start(feat[:, :, :], io["feat"]).then_inc(feat_in, 16)
                sp.dma_start(tabp[:, :, :], io["dft_p"]).then_inc(tabp_in, 16)
                for t in range(TS // P):
                    if t >= 2:
                        pe_t.wait(sp, f"t{t - 2}")
                    sp.dma_start(tab[:, t % 2, :, :], src[:, t, :, :]).then_inc(tab_in[t % 2], 16)
                sp.wait_ge(y_s, 3)
                sp.dma_start(md[0:NP, :, :].rearrange("k p t -> p k t"), y[:, :, :]).then_inc(y_out, 16)
                sp.wait_ge(y_out, 16)

            @block.tensor
            def _(pe):
                pe.wait_ge(feat_in, 16)
                for n in range(NT * 2):
                    t, half = n // 2, n % 2
                    if n >= 8:
                        pe.wait_ge(copied[n % 2], (n - 8) // 2 + 1)
                    for q in range(2):
                        last = pe.matmul(ps[:, n % 8, q * 256:(q + 1) * 256], u[:, half * 2 + q, t * P:(t + 1) * P],
                                         feat[:, 0 if t * P < TS else 1, :], start=True, stop=True)
                    pe_t.did(f"f{n}", last)
                pe.wait_ge(copied[0], NT)
                pe.wait_ge(copied[1], NT)
                pe.wait_ge(tabp_in, 16)
                for j in range(NP):
                    for a in range(2):
                        last = pe.matmul(ps[:, 0, j * TP:(j + 1) * TP], f[:, NT - 1, j, a * P:(a + 1) * P], tabp[:, a, :],
                                         start=a == 0, stop=a == 1)
                pe_t.did("prompt", last)
                pe.wait_ge(y_s, 1)
                for t in range(TS // P):
                    pe.wait_ge(tab_in[t % 2], 16 * (t // 2 + 1))
                    for j in range(NP):
                        for a in range(2):
                            for h in range(2):
                                last = pe.matmul(ps[:, 2 * j + h, :], f[:, t, j, a * P:(a + 1) * P],
                                                 tab[:, t % 2, a, h * 512:(h + 1) * 512],
                                                 start=t == 0 and a == 0, stop=t == TS // P - 1 and a == 1)
                    pe_t.did(f"t{t}", last)

            def copy(eng, half, do):
                for t in range(NT):
                    pe_t.wait(eng, f"f{2 * t + half}")
                    do(f[:, t, half * 2:half * 2 + 2, :], ps[:, (2 * t + half) % 8, :].rearrange("p (q n) -> p q n", q=2))\
                        .then_inc(copied[half], 1)

            @block.vector
            def _(dve):
                copy(dve, 0, dve.tensor_copy)
                pe_t.wait(dve, "prompt")
                dve.tensor_copy(y[:, :, TS:T], ps[:, 0, :].rearrange("p (j n) -> p j n", j=NP)).then_inc(y_s, 1)
                pe_t.wait(dve, f"t{TS // P - 1}")
                dve.tensor_copy(y[:, 0:2, 0:TS].rearrange("p j (h n) -> p j h n", h=2),
                                ps[:, 0:4, :].rearrange("p (j h) n -> p j h n", h=2)).then_inc(y_s, 1)

            @block.scalar
            def _(act):
                copy(act, 1, lambda o, i: act.activation(o, i, ACT.Copy))
                pe_t.wait(act, f"t{TS // P - 1}")
                act.activation(y[:, 2:4, 0:TS].rearrange("p j (h n) -> p j h n", h=2),
                               ps[:, 4:8, :].rearrange("p (j h) n -> p j h n", h=2), ACT.Copy).then_inc(y_s, 1)


def spill(nc, x, xd, back):
    with Stage(nc) as st:
        moved = st.sem("moved")
        with st.block() as block:
            @block.sync
            def _(sp):
                dram = xd.rearrange("k p t -> p k t")
                sp.dma_start(x[:, :, :] if back else dram, dram if back else x[:, :, :]).then_inc(moved, 16)
                sp.wait_ge(moved, 16)


def output_stage(nc, io, sb, md):
    RAW = 2
    x = sb["x"]
    with Stage(nc) as st, nc.psum_tensor("op_ps", [P, 8, 512], F32) as ps, \
            nc.sbuf_tensor("op_m", [P, 2, T], F32) as m, nc.sbuf_tensor("op_hi", [P, KD, T], F32R) as m_hi, \
            nc.sbuf_tensor("op_lo", [P, KD, T], F32R) as m_lo, nc.sbuf_tensor("op_raw", [P, RAW, D], F32) as raw, \
            nc.sbuf_tensor("op_whi", [P, 2, D], F32R) as w_hi, nc.sbuf_tensor("op_wlo", [P, 2, D], F32R) as w_lo:
        m_in, raw_in = [st.sem(f"m_in{n}") for n in range(2)], [st.sem(f"raw_in{n}") for n in range(2)]
        act_t = Steps(st.sem("act_s"), [f"m{k}" for k in range(KD)] + [f"w{o}" for o in range(KD)])
        dve_t = Steps(st.sem("dve_s"), [f"m{k}" for k in range(KD)] + ["w0", "w1"] +
                      [n for o in range(KD) for n in [f"x{o}_{c}" for c in range(NC)] + [f"w{o + 2}"] * (o + 2 < KD)])
        pe_t = Steps(st.sem("pe_s"), [f"o{o}_{c}" for o in range(KD) for c in range(NC)])
        wsrc = io["w_out"][0].rearrange("(k p) n -> p k n", p=P)
        with st.block() as block:
            @block.sync
            def _(sp):
                def load(o):
                    sp.dma_start(raw[:, o % 2, :].rearrange("p (k n) -> p k n", k=KD), wsrc[:, :, o * P:(o + 1) * P])\
                        .then_inc(raw_in[o % 2], 16)
                load(0)
                load(1)
                for k in range(KD):
                    if k >= 2:
                        dve_t.wait(sp, f"m{k - 2}")
                    sp.dma_start(m[:, k % 2, :], md[k, :, :]).then_inc(m_in[k % 2], 16)
                for o in range(2, KD):
                    dve_t.wait(sp, f"w{o - 2}")
                    load(o)

            @block.scalar
            def _(act):
                for k in range(KD):
                    act.wait_ge(m_in[k % 2], 16 * (k // 2 + 1))
                    act_t.did(f"m{k}", act.activation(m_hi[:, k, :], m[:, k % 2, :], ACT.Copy))
                for o in range(KD):
                    act.wait_ge(raw_in[o % 2], 16 * (o // 2 + 1))
                    if o >= 2:
                        pe_t.wait(act, f"o{o - 2}_{NC - 1}")
                    act_t.did(f"w{o}", act.activation(w_hi[:, o % 2, :], raw[:, o % 2, :], ACT.Copy))

            @block.tensor
            def _(pe):
                for o in range(KD):
                    dve_t.wait(pe, f"w{o}")
                    for c in range(NC):
                        cols = slice(c * CW, (c + 1) * CW)
                        n = o * NC + c
                        if n >= 8:
                            dve_t.wait(pe, f"x{(n - 8) // NC}_{(n - 8) % NC}")
                        for k in range(KD):
                            ks = slice(k * P, (k + 1) * P)
                            last = mm3(pe, ps[:, n % 8, 0:CW], w_hi[:, o % 2, ks], w_lo[:, o % 2, ks],
                                       m_hi[:, k, cols], m_lo[:, k, cols], k == 0, k == KD - 1)
                        pe_t.did(f"o{o}_{c}", last)

            @block.vector
            def _(dve):
                for k in range(KD):
                    act_t.wait(dve, f"m{k}")
                    dve_t.did(f"m{k}", dve.tensor_tensor(m_lo[:, k, :], m[:, k % 2, :], m_hi[:, k, :].bitcast(F32), ALU.subtract))

                def lower(o):
                    act_t.wait(dve, f"w{o}")
                    dve_t.did(f"w{o}", dve.tensor_tensor(w_lo[:, o % 2, :], raw[:, o % 2, :],
                                                         w_hi[:, o % 2, :].bitcast(F32), ALU.subtract))
                lower(0)
                lower(1)
                for o in range(KD):
                    for c in range(NC):
                        pe_t.wait(dve, f"o{o}_{c}")
                        for s, a, b in parts(c):
                            xs = x[:, o, c * CW + a:c * CW + b]
                            last = dve.scalar_tensor_tensor(xs, ps[:, (o * NC + c) % 8, a:b],
                                                            sb["mod"][:, 5 * KD + o, s:s + 1], xs, ALU.mult, ALU.add)
                        dve_t.did(f"x{o}_{c}", last)
                    if o + 2 < KD:
                        lower(o + 2)


class Rwkv:

    def __init__(self, nc, ctx):
        def sbuf(name, shape, dt=F32):
            return ctx.enter_context(nc.sbuf_tensor("rw_" + name, shape, dt))
        self.lora = sbuf("lora", [P, 3, T])
        self.reset = sbuf("reset", [P, T], BF16)
        self.w2, self.a2, self.g2 = sbuf("w2", [P, P]), sbuf("a2", [P, P]), sbuf("g2", [P, P])
        self.pp = sbuf("pp", [P, 10])
        self.rkv = sbuf("rkv", [P, 3, T])
        self.ar = sbuf("ar", [P, 2, 2, T])
        self.bk = sbuf("bk", [P, 2, NCH, 2, HS])
        self.gr = sbuf("gr", [P, 2, 2, NCH, 2 * HS])
        self.bt = sbuf("bt", [P, 2, NCH, P])
        self.sv = sbuf("sv", [P, 2, 2, NCH, HS])
        self.wt = sbuf("wt", [HS, 2, 2, NCH, HS])
        self.work = sbuf("work", [P, 6144])
        self.pc = sbuf("pc", [P, 2, NCH])
        self.m = sbuf("m", [P, 2, 2, HS])
        self.mp = sbuf("mp", [P, 2, HS])
        self.m0 = sbuf("m0", [P, 2, HS])
        self.st = sbuf("st", [P, 2, HS])
        g = self.gr[:, :, :, :, :].rearrange("p d h c n -> p (d h c n)")
        self.t = [g[:, n * T:(n + 1) * T] for n in range(8)] + [self.work[:, n * T:(n + 1) * T] for n in range(5)]


PP = {n: i for i, n in enumerate(("w0_0", "w0_1", "a0_0", "a0_1", "k_k", "k_a", "r_k", "ln_w", "ln_b", "one_ka"))}


def rw_setup(nc, io, sb, rw, zd):
    with Stage(nc) as st:
        lora_in, own, ones = st.sem("lora_in"), st.sem("own"), st.sem("ones")
        with st.block() as block:
            @block.sync
            def _(sp):
                sp.dma_start(rw.lora[:, :, :], zd[NZ - 3:NZ, :, :].rearrange("k p t -> p k t")).then_inc(lora_in, 16)

            @block.scalar
            def _(act):
                act.wait_ge(lora_in, 16)
                act.activation(rw.lora[:, 0, :], rw.lora[:, 0, :], ACT.Tanh)
                act.activation(rw.lora[:, 2, :], rw.lora[:, 2, :], ACT.Sigmoid).then_inc(own, 1)

            @block.vector
            def _(dve):
                dve.memset(rw.reset[:, :], 1.0).then_inc(ones, 1)
                dve.wait_ge(ones, 1)
                dve.memset(rw.reset[:, ::HS], 0.0).then_inc(ones, 1)


def rw_features(nc, io, sb, rw, zd, p):
    with Stage(nc) as st, nc.psum_tensor("e_ps", [P, 8, 512], F32) as ps:
        z_in, w_in, s_in = [st.sem(f"z_in{n}") for n in range(3)], [st.sem(f"w_in{n}") for n in range(3)], st.sem("s_in")
        act_t = Steps(st.sem("act_s"), ["kraw", "sq", "sig_w0", "sig_a0", "sig_w1", "sig_a1", "sqrt"] +
                      [f"{n}{d}" for d in range(2) for n in ("P", "iP", "kda", "Pp")])
        dve_t = Steps(st.sem("dve_s"), ["pp", "ka1", "ss", "inv", "kk"] +
                      [f"{n}{d}" for d in range(2) for n in ("scan", "Lp", "pc", "R", "ak", "B", "A", "kd", "K")] +
                      ["kds", "rkk", "bonus"])
        pe_t = Steps(st.sem("pe_s"), ["ss", "w0", "a0", "w1", "a1", "bonus"])
        r, k, v = (rw.rkv[:, n, :] for n in range(3))
        kk, sq, sw, ai, lc, e1, e2, e3 = rw.t[0], rw.t[1], rw.t[2:4], rw.t[4:6], rw.t[6:8], rw.t[8:10], rw.t[10:12], rw.t[12]
        b3 = lambda t: t.rearrange("p (c n) -> p c n", c=NC)
        lo, hi = ps[:, 0:3, 0:CW], ps[:, 3:6, 0:CW]
        pp = lambda n: rw.pp[:, PP[n]:PP[n] + 1]
        by_chunk = lambda t: t.rearrange("p (c n) -> p c n", c=NCH)
        rev = lambda t, d: t[:, ::-1] if d else t
        end = lambda t, d: t[:, 0::HS] if d else t[:, HS - 1::HS]
        with st.block() as block:
            @block.sync
            def _(sp):
                for n in (1, 0, 2):
                    sp.dma_start(rw.rkv[:, n, :], zd[bass.ds(p + 4 * n, 1), :, :].rearrange("a p t -> p (a t)"))\
                      .then_inc(z_in[n], 16)
                    if n == 1:
                        cols = bass.ds(p * P, P)
                        sp.dma_start(rw.w2[:, :], io["decay_w2"][0].rearrange("d i n -> (d i) n")[:, cols]).then_inc(w_in[0], 16)
                        sp.dma_start(rw.a2[:, :], io["iclr_a2"][0].rearrange("d i n -> (d i) n")[:, cols]).then_inc(w_in[1], 16)
                        sp.dma_start(rw.g2[:, :], io["gate_g2"][0][:, cols]).then_inc(w_in[2], 16)
                for d, name in enumerate(("state_fwd", "state_bwd")):
                    sp.dma_start(rw.st[:, d, :], io[name][0, 0, bass.ds(p * 2, 2), :, :].rearrange("h v k -> (h v) k"))\
                        .then_inc(s_in, 16)
                sp.wait_ge(w_in[2], 16)
                sp.wait_ge(s_in, 32)

            @block.tensor
            def _(pe):
                blk = sb["cst"][:, C_BLK:C_BLK + P]

                def over(name, out, w, x):
                    for c in range(NC):
                        last = pe.matmul(out[:, c, :], w, x[:, c * CW:(c + 1) * CW], start=True, stop=True)
                    pe_t.did(name, last)
                act_t.wait(pe, "sq")
                over("ss", lo, blk, sq)
                for d in range(2):
                    rows = slice(HS * d, HS * d + HS)
                    pe.wait_ge(w_in[0], 16)
                    if d:
                        act_t.wait(pe, "sig_w0")
                    over(f"w{d}", hi, rw.w2[rows, :], rw.lora[rows, 0, :])
                    pe.wait_ge(w_in[1], 16)
                    if d:
                        act_t.wait(pe, "sig_a0")
                    else:
                        dve_t.wait(pe, "ss")
                    over(f"a{d}", lo, rw.a2[rows, :], rw.lora[rows, 1, :])
                dve_t.wait(pe, "rkk")
                act_t.wait(pe, "sig_a1")
                over("bonus", lo, blk, sq)

            @block.scalar
            def _(act):
                act.wait_ge(z_in[1], 16)
                dve_t.wait(act, "ka1")
                act_t.did("kraw", act.activation(kk, k, ACT.Identity, scale=pp("k_k")))
                act_t.wait(act, "kraw")
                act_t.did("sq", act.activation(sq, kk, ACT.Square))
                for d in range(2):
                    pe_t.wait(act, f"w{d}")
                    act_t.did(f"sig_w{d}", act.activation(b3(sw[d]), hi, ACT.Sigmoid, bias=pp(f"w0_{d}")))
                    pe_t.wait(act, f"a{d}")
                    act_t.did(f"sig_a{d}", act.activation(b3(ai[d]), lo, ACT.Sigmoid, bias=pp(f"a0_{d}")))
                dve_t.wait(act, "ss")
                act_t.did("sqrt", act.activation(sq, sq, ACT.Sqrt))
                for d in range(2):
                    dve_t.wait(act, f"scan{d}")
                    act_t.did(f"P{d}", act.activation(e1[d], lc[d], ACT.Exp, scale=-DECAY))
                    act_t.did(f"iP{d}", act.activation(e2[d], lc[d], ACT.Exp, scale=DECAY))
                    dve_t.wait(act, f"Lp{d}")
                    act_t.did(f"kda{d}", act.activation(sw[d], ai[d], ACT.Identity, bias=pp("one_ka"), scale=pp("k_a")))
                    act_t.wait(act, f"iP{d}")
                    act_t.did(f"Pp{d}", act.activation(lc[d], lc[d], ACT.Exp, scale=-DECAY))

            @block.vector
            def _(dve):
                at = PRM["w0"][0]
                dve_t.did("pp", dve.tensor_copy(
                    rw.pp[:, 0:9].unsqueeze(2),
                    sb["prm"][:, at:at + 36].rearrange("p (n f) -> p n f", f=4)[:, :, bass.ds(p, 1)]))
                dve_t.wait(dve, "pp")
                dve_t.did("ka1", dve.tensor_scalar(pp("one_ka"), pp("k_a"), -1.0, 1.0, ALU.mult, ALU.add))
                pe_t.wait(dve, "ss")
                dve_t.did("ss", dve.tensor_scalar(b3(sq), lo, 1e-24, None, ALU.max))
                act_t.wait(dve, "sqrt")
                dve_t.did("inv", dve.reciprocal(sq, sq))
                dve_t.wait(dve, "inv")
                dve_t.did("kk", dve.tensor_tensor(kk, kk, sq, ALU.mult))
                dve.wait_ge(z_in[0], 16)
                for d in range(2):
                    act_t.wait(dve, f"sig_w{d}")
                    dve_t.did(f"scan{d}", dve.tensor_tensor_scan(rev(lc[d], d), rw.reset[:, :], rev(sw[d], d), 0.0,
                                                                 ALU.mult, ALU.add))
                    act_t.wait(dve, f"iP{d}")
                    dve_t.did(f"Lp{d}", dve.tensor_tensor(lc[d], lc[d], sw[d], ALU.subtract))
                    dve_t.did(f"pc{d}", dve.tensor_copy(rw.pc[:, d, :], end(e1[d], d)))
                    dve_t.did(f"R{d}", dve.tensor_tensor(rw.ar[:, d, 1, :], r, e1[d], ALU.mult))
                    dve_t.wait(dve, "kk")
                    dve_t.did(f"ak{d}", dve.tensor_tensor(e3, ai[d], kk, ALU.mult))
                    dve_t.wait(dve, f"ak{d}")
                    dve_t.did(f"B{d}", dve.tensor_tensor(rw.bk[:, d, :, 0, :], by_chunk(e3), by_chunk(e2[d]), ALU.mult))
                    act_t.wait(dve, f"Pp{d}")
                    dve_t.did(f"A{d}", dve.tensor_tensor(rw.ar[:, d, 0, :], kk, lc[d], ALU.mult))
                    dve_t.did(f"kd{d}", dve.tensor_tensor(sw[d], sw[d], k, ALU.mult))
                    dve_t.wait(dve, f"kd{d}")
                    dve_t.did(f"K{d}", dve.tensor_tensor(rw.bk[:, d, :, 1, :], by_chunk(sw[d]), by_chunk(e2[d]), ALU.mult))
                dve_t.did("kds", dve.tensor_tensor(sq, sw[0], sw[1], ALU.add))
                dve_t.wait(dve, "kds")
                dve_t.did("rkk", dve.scalar_tensor_tensor(sq, sq, pp("r_k"), r, ALU.mult, ALU.mult))
                pe_t.wait(dve, "bonus")
                dve.wait_ge(z_in[2], 16)
                dve_t.did("bonus", dve.tensor_tensor(b3(r), lo, b3(v), ALU.mult))


def rw_grams(nc, io, sb, rw):
    GC = 3
    NG = NCH // GC
    with Stage(nc) as st, nc.psum_tensor("g_ps", [P, 8, 512], F32) as ps:
        order = [(d, g) for d in range(2) for g in range(NG)]
        rkv = rw.rkv[:, :, :].rearrange("p n t -> p (n t)")
        pe_t = Steps(st.sem("pe_s"), [x for n in range(2 * NG) for x in ([f"g{n}", f"b{n}"] + [f"v{n}"] * (n < NG))] + ["m0"])
        dve_t = Steps(st.sem("dve_s"), [f"g{n}" for n in range(2 * NG)] + ["m0"])
        act_t = Steps(st.sem("act_s"), [x for n in range(2 * NG) for x in ([f"b{n}"] + [f"v{n}"] * (n < NG))])
        ident = sb["cst"][:, C_ID:C_ID + P]
        with st.block() as block:
            @block.tensor
            def _(pe):
                for n, (d, g) in enumerate(order):
                    if n >= 2:
                        dve_t.wait(pe, f"g{n - 2}")
                    for h in range(2):
                        rows = slice(HS * h, HS * h + HS)
                        for j in range(GC):
                            c = g * GC + j
                            cols = slice(c * HS, (c + 1) * HS)
                            last = pe.matmul(ps[:, n % 2 * 2 + h, j * P:(j + 1) * P], rw.bk[rows, d, c, :, :].rearrange("p b n -> p (b n)"),
                                             rw.ar[rows, d, :, cols], start=True, stop=True)
                    pe_t.did(f"g{n}", last)
                    if n >= 2:
                        act_t.wait(pe, f"b{n - 2}")
                    for j in range(GC):
                        c = g * GC + j
                        last = pe.transpose(ps[:, 4 + n % 2, j * P:(j + 1) * P], rw.bk[:, d, c, :, :].rearrange("p b n -> p (b n)"), ident)
                    pe_t.did(f"b{n}", last)
                    if n < NG:
                        if n >= 2:
                            act_t.wait(pe, f"v{n - 2}")
                        for j in range(GC):
                            c = g * GC + j
                            last = pe.transpose(ps[:, 6 + n % 2, j * P:(j + 1) * P],
                                                rkv[:, 2 * T + (c - 1) * HS:2 * T + (c + 1) * HS], ident)
                        pe_t.did(f"v{n}", last)
                act_t.wait(pe, f"v{NG - 1}")
                for h in range(2):
                    rows = slice(HS * h, HS * h + HS)
                    for d in range(2):
                        last = pe.matmul(ps[rows, 6 + h, d * HS:(d + 1) * HS], rw.st[rows, d, :],
                                         ident[rows, HS * h:HS * h + HS], start=True, stop=True)
                pe_t.did("m0", last)

            @block.vector
            def _(dve):
                for n, (d, g) in enumerate(order):
                    pe_t.wait(dve, f"g{n}")
                    mask = sb["cst"][:, C_MASK + d * P:C_MASK + (d + 1) * P].unsqueeze(1).to_broadcast([P, GC, P])
                    for h in range(2):
                        last = dve.tensor_tensor(rw.gr[:, d, h, g * GC:(g + 1) * GC, :],
                                                 ps[:, n % 2 * 2 + h, 0:GC * P].rearrange("p (c n) -> p c n", c=GC), mask, ALU.mult)
                    dve_t.did(f"g{n}", last)
                pe_t.wait(dve, "m0")
                for h in range(2):
                    rows = slice(HS * h, HS * h + HS)
                    last = dve.tensor_copy(rw.m0[rows, :, :], ps[rows, 6 + h, 0:P].rearrange("p (d n) -> p d n", d=2))
                dve_t.did("m0", last)

            @block.scalar
            def _(act):
                for n, (d, g) in enumerate(order):
                    pe_t.wait(act, f"b{n}")
                    act_t.did(f"b{n}", act.activation(rw.bt[:, d, g * GC:(g + 1) * GC, :],
                                                      ps[:, 4 + n % 2, 0:GC * P].rearrange("p (c n) -> p c n", c=GC), ACT.Copy))
                    if n < NG:
                        pe_t.wait(act, f"v{n}")
                        for dd in range(2):
                            for h in range(2):
                                last = act.activation(
                                    rw.sv[HS:P, dd, h, g * GC:(g + 1) * GC, :],
                                    ps[HS:P, 6 + n % 2, 0:GC * P].rearrange("p (c h n) -> p h c n", c=GC, h=2)[:, h], ACT.Copy)
                        act_t.did(f"v{n}", last)


def rw_invert(nc, io, sb, rw, nd, wd):
    B = 32
    U = 4 * NCH // 2
    GC = 4
    with Stage(nc) as st, nc.psum_tensor("i_ps", [P, 4, 512], F32) as ps:
        work = rw.work
        nt = work[0:HS, 0:U * B].rearrange("p (u t) -> p u t", u=U)
        ni = work[0:2 * U, 2048:4096].rearrange("p (b i j) -> p b i j", b=2, i=B)
        wi = work[0:2 * U, 4096:6144].rearrange("p (b i j) -> p b i j", b=2, i=B)
        tmp = work[0:2 * U, 0:2048].rearrange("p (b i j) -> p b i j", b=2, i=B)
        gu = rw.gr[:, :, :, :, :].rearrange("p d h c n -> p d (h c) n")
        n_out, n_in, w_out, own = st.sem("n_out"), st.sem("n_in"), st.sem("w_out"), st.sem("own")
        tr, zero, a_turned, a_copied = st.sem("tr"), st.sem("zero"), st.sem("a_turned"), st.sem("a_copied")
        tw_in, tw_s = st.sem("tw_in"), st.sem("tw_s")
        tw = work[0:HS, 0:2 * U * B].rearrange("p (u t) -> p u t", u=2 * U)
        twt = work[0:HS, 2 * U * B:4 * U * B].rearrange("p (u t) -> p u t", u=2 * U)
        with st.block() as block:
            @block.sync
            def _(sp):
                for b in range(2):
                    rows = slice(B * b, B * b + B)
                    sp.dma_start(nd[0:U, b].rearrange("u r t -> r u t"), gu[rows, 0, :, rows]).then_inc(n_out, 16)
                sp.wait_ge(tr, 2)
                for b in range(2):
                    sp.dma_start(nd[U:2 * U, b].rearrange("u r t -> r u t"), nt[B * b:B * b + B, :, :]).then_inc(n_out, 16)
                sp.wait_ge(n_out, 64)
                sp.dma_start(ni.rearrange("p b i j -> p (b i j)"), nd.rearrange("u b r t -> u (b r t)")).then_inc(n_in, 16)
                sp.wait_ge(own, 2 + 2 * (B - 1))
                sp.dma_start(wd.rearrange("u b r t -> u (b r t)"), wi.rearrange("p b i j -> p (b i j)")).then_inc(w_out, 16)
                sp.wait_ge(w_out, 16)
                for b in range(2):
                    sp.dma_start(tw[B * b:B * b + B, :, :], wd[:, b].rearrange("u r t -> r u t")).then_inc(tw_in, 16)
                sp.wait_ge(tw_in, 32)

            @block.gpsimd
            def _(pool):
                for d in range(2):
                    pool.memset(rw.wt[:, d, :, :, :], 0.0).then_inc(zero, 1)

            @block.vector
            def _(dve):
                for b in range(2):
                    rows = slice(B * b, B * b + B)
                    dve.transpose(nt[rows, :, :], gu[rows, 1, :, rows]).then_inc(tr, 1)
                dve.memset(wi, 0.0).then_inc(own, 1)
                dve.wait_ge(own, 1)
                dve.memset(wi.rearrange("p b i j -> p b (i j)")[:, :, ::B + 1], 1.0).then_inc(own, 1)
                dve.wait_ge(n_in, 16)
                n = 2
                for j in range(B - 1, 0, -1):
                    dve.wait_ge(own, n)
                    sh = [2 * U, 2, j, B - j]
                    t = tmp[:, :, 0:j, j:B]
                    dve.tensor_tensor(t, ni[:, :, 0:j, j:j + 1].to_broadcast(sh), wi[:, :, j:j + 1, j:B].to_broadcast(sh),
                                      ALU.mult).then_inc(own, 1)
                    dve.wait_ge(own, n + 1)
                    dve.tensor_tensor(wi[:, :, 0:j, j:B], wi[:, :, 0:j, j:B], t, ALU.subtract).then_inc(own, 1)
                    n += 2
                dve.wait_ge(tw_in, 32)
                dve.transpose(twt[:, :, :], tw[:, :, :]).then_inc(tw_s, 1)
                dve.wait_ge(tw_s, 1)
                dve.wait_ge(zero, 2)
                for d in range(2):
                    for b in range(2):
                        rows = slice(B * b, B * b + B)
                        src = tw if d == 0 else twt
                        dve.tensor_copy(rw.wt[rows, d, :, :, rows].rearrange("p h c t -> p (h c) t"),
                                        src[rows, d * U:(d + 1) * U, :]).then_inc(tw_s, 1)

            @block.tensor
            def _(pe):
                n = 0
                for d in range(2):
                    for c in range(NCH):
                        if n >= GC and n % GC == 0 and n // GC >= 4:
                            pe.wait_ge(a_copied, n // GC - 3)
                        last = pe.transpose(ps[0:HS, n // GC % 4, n % GC * P:(n % GC + 1) * P],
                                            rw.ar[:, d, 0, c * HS:(c + 1) * HS], sb["cst"][:, C_ID:C_ID + P])
                        n += 1
                        if n % GC == 0:
                            last.then_inc(a_turned, 1)

            @block.scalar
            def _(act):
                at = rw.bk[0:HS, :, :, :, :].rearrange("p d c b n -> p (d c b n)")
                for g in range(2 * NCH // GC):
                    act.wait_ge(a_turned, g + 1)
                    act.activation(at[:, g * GC * P:(g + 1) * GC * P], ps[0:HS, g % 4, :], ACT.Copy).then_inc(a_copied, 1)


def rw_solve(nc, sb, rw):
    B = 32
    U = 2 * NCH
    GU = 12
    with Stage(nc) as st, nc.psum_tensor("s_ps", [P, 8, 512], F32) as ps:
        work = rw.work
        tw = work[0:HS, 0:2 * U * B].rearrange("p (u t) -> p u t", u=2 * U)
        twt = work[0:HS, 2 * U * B:4 * U * B].rearrange("p (u t) -> p u t", u=2 * U)
        fs = work[0:HS, 4 * U * B:5 * U * B]
        gu = rw.gr[:, :, :, :, :].rearrange("p d h c n -> p d (h c) n")
        wu = rw.wt[:, :, :, :, :].rearrange("p d h c n -> p d (h c) n")
        su = rw.sv[:, :, :, :, :].rearrange("p d h c n -> p d (h c) n")
        zg = work[0:HS, 0:2 * U * HS].rearrange("p (d u n) -> p d u n", d=2, u=U)
        at = rw.bk[0:HS, :, :, :, :].rearrange("p d c b n -> p d c (b n)")
        NB = 2 * U // 8
        pe_t = Steps(st.sem("pe_s"), ["f0", "f1", "w0", "w1"] + [f"z{n}" for n in range(NB)] + [f"u{n}" for n in range(NB)] +
                     [f"a{n}" for n in range(6)])
        dve_t = Steps(st.sem("dve_s"), ["f0", "w0"] + [f"z{n}" for n in range(0, NB, 2)] + [f"u{n}" for n in range(0, NB, 2)] +
                      [f"a{n}" for n in range(0, 6, 2)])
        act_t = Steps(st.sem("act_s"), ["f1", "w1"] + [f"z{n}" for n in range(1, NB, 2)] + [f"u{n}" for n in range(1, NB, 2)] +
                      [f"a{n}" for n in range(1, 6, 2)])
        both = lambda n: dve_t if n % 2 == 0 else act_t
        first = lambda d: slice(0, B) if d == 0 else slice(B, HS)
        second = lambda d: slice(B, HS) if d == 0 else slice(0, B)
        with st.block() as block:
            @block.tensor
            def _(pe):
                for d in range(2):
                    nat = twt if d == 0 else tw
                    for u in range(U):
                        q = 4 * d + u // GU
                        last = pe.matmul(ps[second(d), q, u % GU * B:(u % GU + 1) * B], gu[first(d), d, u, second(d)],
                                         nat[first(d), d * U + u, :], start=True, stop=True)
                    pe_t.did(f"f{d}", last)
                for d in range(2):
                    both(d).wait(pe, f"f{d}")
                    for u in range(U):
                        q = 4 * d + u // GU
                        last = pe.matmul(ps[first(d), q, u % GU * B:(u % GU + 1) * B], fs[second(d), u * B:(u + 1) * B],
                                         wu[second(d), d, u, second(d)], start=True, stop=True)
                    pe_t.did(f"w{d}", last)
                both(0).wait(pe, "w0")
                both(1).wait(pe, "w1")
                for n in range(NB):
                    if n >= 8:
                        both(n).wait(pe, f"z{n - 8}")
                    for i in range(8):
                        d, u = (8 * n + i) // U, (8 * n + i) % U
                        last = pe.matmul(ps[0:HS, n % 8, i * HS:(i + 1) * HS], gu[HS:P, d, u, 0:HS], su[HS:P, d, u, :],
                                         start=True, stop=True)
                    pe_t.did(f"z{n}", last)
                for n in range(NB):
                    both(n).wait(pe, f"z{n}")
                    m = n + NB
                    if n < 8:
                        both(n + 1).wait(pe, f"z{n + 1}") if n + 1 < NB else None
                        if m - 8 < NB:
                            both(m - 8).wait(pe, f"z{m - 8}")
                    else:
                        both(n - 8).wait(pe, f"u{n - 8}")
                        both(n - 9).wait(pe, f"u{n - 9}") if n >= 9 else both(NB - 1).wait(pe, f"z{NB - 1}")
                    for i in range(8):
                        d, u = (8 * n + i) // U, (8 * n + i) % U
                        last = pe.matmul(ps[0:HS, m % 8, i * HS:(i + 1) * HS], wu[:, d, u, :], zg[:, d, u, :],
                                         start=True, stop=True)
                    pe_t.did(f"u{n}", last)
                both(NB - 1).wait(pe, f"u{NB - 1}")
                both(NB - 2).wait(pe, f"u{NB - 2}")
                for n in range(6):
                    for i in range(6):
                        d, c = n // 3, n % 3 * 6 + i
                        for h in range(2):
                            last = pe.matmul(ps[HS * h:HS * h + HS, n, i * HS:(i + 1) * HS], at[:, d, c, HS * h:HS * h + HS],
                                             rw.wt[:, d, h, c, :], start=True, stop=True)
                    pe_t.did(f"a{n}", last)

            def evac(eng, tr, par, copy, neg):
                d = par
                fv = fs.rearrange("p (q n) -> p q n", q=3)
                pe_t.wait(eng, f"f{d}")
                tr.did(f"f{d}", copy(fv[second(d)], ps[second(d), 4 * d:4 * d + 3, 0:GU * B]))
                pe_t.wait(eng, f"w{d}")
                for q in range(3):
                    last = neg(wu[first(d), d, q * GU:(q + 1) * GU, second(d)],
                               ps[first(d), 4 * d + q, 0:GU * B].rearrange("p (u n) -> p u n", u=GU))
                tr.did(f"w{d}", last)
                zf = zg.rearrange("p d u n -> p (d u n)")
                for n in range(par, NB, 2):
                    pe_t.wait(eng, f"z{n}")
                    if n < 2:
                        pe_t.wait(eng, "w1")
                    tr.did(f"z{n}", copy(zf[:, n * 512:(n + 1) * 512], ps[0:HS, n % 8, :]))
                gf = rw.gr[:, :, :, :, :].rearrange("p d h c n -> p (d h c) n")
                for n in range(par, NB, 2):
                    pe_t.wait(eng, f"u{n}")
                    tr.did(f"u{n}", neg(gf[0:HS, 8 * n:8 * n + 8, 0:HS],
                                        ps[0:HS, (n + NB) % 8, :].rearrange("p (u n) -> p u n", u=8)))
                for n in range(par, 6, 2):
                    pe_t.wait(eng, f"a{n}")
                    d, c = n // 3, n % 3 * 6
                    tr.did(f"a{n}", neg(rw.ar[:, d, 0, c * HS:(c + 6) * HS], ps[:, n, 0:6 * HS]))

            @block.vector
            def _(dve):
                evac(dve, dve_t, 0, dve.tensor_copy, lambda o, i: dve.tensor_scalar(o, i, -1.0, None, ALU.mult))

            @block.scalar
            def _(act):
                evac(act, act_t, 1, lambda o, i: act.activation(o, i, ACT.Copy),
                     lambda o, i: act.activation(o, i, ACT.Copy, scale=-1.0))


def rw_scan(nc, io, sb, rw, p):
    order = [list(range(SCH, NCH)) + list(range(SCH)), list(range(NCH - 1, SCH - 1, -1)) + list(range(SCH - 1, -1, -1))]
    NPC = NCH - SCH
    SD = [(i, d) for i in range(NCH) for d in range(2)]
    y = [rw.work[:, d * T:(d + 1) * T] for d in range(2)]
    with Stage(nc) as st, nc.psum_tensor("c_ps", [P, 8, 512], F32) as ps:
        pe_t = Steps(st.sem("pe_s"), [x for i in range(NCH) for x in (f"S{i}_0", f"S{i}_1", f"M{i}_0", f"Y{i}_0", f"M{i}_1", f"Y{i}_1")] +
                     ["st0", "st1"])
        dve_t = Steps(st.sem("dve_s"), ["zero"] + [x for i in range(NCH) for x in
                                                   [f"S{i}_0", f"S{i}_1"] + [f"M{i}_0", f"M{i}_1"]])
        act_t = Steps(st.sem("act_s"), [f"Y{i}_{d}" for i, d in SD] + ["st0", "st1"])
        pool_t = Steps(st.sem("pool_s"), [f"mp{i}_{d}" for i, d in SD])
        out_s = st.sem("out_s")
        old = lambda i, d: rw.m0[:, d, :] if i == NPC else rw.m[:, i % 2, d, :]
        with st.block() as block:
            @block.tensor
            def _(pe):
                def s_part(i, d):
                    c = order[d][i]
                    dve_t.wait(pe, f"M{i - 1}_{d}" if i else "zero")
                    if i:
                        act_t.wait(pe, f"Y{i - 1}_{d}")
                    for h in range(2):
                        rows = slice(HS * h, HS * h + HS)
                        last = pe.matmul(ps[0:HS, 2 * d + h, 0:HS], rw.ar[rows, d, 0, c * HS:(c + 1) * HS],
                                         old(i, d)[rows], start=True, stop=True)
                    pe_t.did(f"S{i}_{d}", last)

                def rest(i, d):
                    c = order[d][i]
                    dve_t.wait(pe, f"S{i}_{d}")
                    for h in range(2):
                        rows = slice(HS * h, HS * h + HS)
                        last = pe.matmul(ps[rows, 4 + d, 0:HS], rw.bt[:, d, c, HS * h:HS * h + HS],
                                         rw.sv[:, d, h, c, :], start=True, stop=True)
                    pe_t.did(f"M{i}_{d}", last)
                    for h in range(2):
                        rows = slice(HS * h, HS * h + HS)
                        pe.matmul(ps[rows, 2 * d + h, HS:2 * HS], rw.sv[:, d, h, c, :], rw.gr[:, d, h, c, HS:2 * HS],
                                  start=True, stop=False)
                    for h in range(2):
                        rows = slice(HS * h, HS * h + HS)
                        last = pe.matmul(ps[rows, 2 * d + h, HS:2 * HS], old(i, d)[rows],
                                         rw.ar[rows, d, 1, c * HS:(c + 1) * HS], start=False, stop=True)
                    pe_t.did(f"Y{i}_{d}", last)
                for i, d in SD:
                    s_part(i, d)
                    if d:
                        rest(i, 0)
                        rest(i, 1)
                for d in range(2):
                    act_t.wait(pe, f"Y{NCH - 1}_{d}")
                    for h in range(2):
                        rows = slice(HS * h, HS * h + HS)
                        last = pe.matmul(ps[rows, 2 * d + h, HS:2 * HS], rw.st[rows, d, :],
                                         sb["cst"][rows, C_ID + HS * h:C_ID + HS * h + HS], start=True, stop=True)
                    pe_t.did(f"st{d}", last)

            @block.vector
            def _(dve):
                dve_t.did("zero", dve.memset(rw.m[:, 0, :, :], 0.0))
                for i in range(NCH):
                    for d in range(2):
                        c = order[d][i]
                        pe_t.wait(dve, f"S{i}_{d}")
                        dve_t.did(f"S{i}_{d}", dve.tensor_tensor(rw.sv[0:HS, d, :, c, :], ps[0:HS, 2 * d:2 * d + 2, 0:HS],
                                                                 rw.gr[0:HS, d, :, c, 0:HS], ALU.add))
                    for d in range(2):
                        c = order[d][i]
                        new = rw.st[:, d, :] if i == NPC - 1 else rw.m[:, (i + 1) % 2, d, :]
                        pe_t.wait(dve, f"M{i}_{d}")
                        pool_t.wait(dve, f"mp{i}_{d}")
                        dve_t.did(f"M{i}_{d}", dve.scalar_tensor_tensor(new, ps[:, 4 + d, 0:HS], rw.pc[:, d, c:c + 1],
                                                                       rw.mp[:, d, :], ALU.mult, ALU.add))

            @block.gpsimd
            def _(pool):
                for i, d in SD:
                    c = order[d][i]
                    if i:
                        dve_t.wait(pool, f"M{i - 1}_{d}")
                    else:
                        dve_t.wait(pool, "zero")
                    pool_t.did(f"mp{i}_{d}", pool.tensor_scalar(rw.mp[:, d, :], old(i, d), rw.pc[:, d, c:c + 1], None, ALU.mult))

            @block.scalar
            def _(act):
                for i, d in SD:
                    c = order[d][i]
                    pe_t.wait(act, f"Y{i}_{d}")
                    for h in range(2):
                        rows = slice(HS * h, HS * h + HS)
                        last = act.activation(y[d][rows, c * HS:(c + 1) * HS], ps[rows, 2 * d + h, HS:2 * HS], ACT.Copy)
                    act_t.did(f"Y{i}_{d}", last)
                for d in range(2):
                    pe_t.wait(act, f"st{d}")
                    dve_t.wait(act, f"M{NCH - 1}_{d}")
                    for h in range(2):
                        rows = slice(HS * h, HS * h + HS)
                        last = act.activation(rw.mp[rows, d, :], ps[rows, 2 * d + h, HS:2 * HS], ACT.Copy)
                    act_t.did(f"st{d}", last)

            @block.sync
            def _(sp):
                for d, name in enumerate(("state_f", "state_b")):
                    act_t.wait(sp, f"st{d}")
                    sp.dma_start(io[name][0, 0, bass.ds(p * 2, 2), :, :].rearrange("h v k -> (h v) k"), rw.mp[:, d, :])\
                      .then_inc(out_s, 16)
                sp.wait_ge(out_s, 32)


def rw_finish(nc, sb, rw, md, p):
    y, yb, c2, rs = (rw.work[:, n * T:(n + 1) * T] for n in range(4))
    b3 = lambda t: t.rearrange("p (c n) -> p c n", c=NC)
    pp = lambda n: rw.pp[:, PP[n]:PP[n] + 1]
    with Stage(nc) as st, nc.psum_tensor("p_ps", [P, 8, 512], F32) as ps:
        lo, hi = ps[:, 0:3, 0:CW], ps[:, 3:6, 0:CW]
        pe_t = Steps(st.sem("pe_s"), ["mean", "gate", "var"])
        dve_t = Steps(st.sem("dve_s"), ["y", "centre", "var", "rstd", "norm", "bonus", "gate"])
        act_t = Steps(st.sem("act_s"), ["sq", "sqrt", "affine"])
        y_out = st.sem("y_out")
        with st.block() as block:
            @block.tensor
            def _(pe):
                def over(name, out, w, x):
                    for c in range(NC):
                        last = pe.matmul(out[:, c, :], w, x[:, c * CW:(c + 1) * CW], start=True, stop=True)
                    pe_t.did(name, last)
                blk = sb["cst"][:, C_BLK:C_BLK + P]
                dve_t.wait(pe, "y")
                over("mean", lo, blk, y)
                over("gate", hi, rw.g2[:, :], rw.lora[:, 2, :])
                act_t.wait(pe, "sq")
                over("var", lo, blk, c2)

            @block.vector
            def _(dve):
                dve_t.did("y", dve.tensor_tensor(y, y, yb, ALU.add))
                pe_t.wait(dve, "mean")
                dve_t.did("centre", dve.scalar_tensor_tensor(b3(y), lo, -1.0 / HS, b3(y), ALU.mult, ALU.add))
                pe_t.wait(dve, "var")
                dve_t.did("var", dve.tensor_scalar(b3(rs), lo, 1.0 / HS, GN_EPS, ALU.mult, ALU.add))
                act_t.wait(dve, "sqrt")
                dve_t.did("rstd", dve.reciprocal(rs, rs))
                dve_t.wait(dve, "rstd")
                dve_t.did("norm", dve.tensor_tensor(y, y, rs, ALU.mult))
                act_t.wait(dve, "affine")
                dve_t.did("bonus", dve.tensor_tensor(y, y, rw.rkv[:, 0, :], ALU.add))
                dve_t.wait(dve, "bonus")
                dve_t.did("gate", dve.tensor_tensor(b3(y), hi, b3(y), ALU.mult))

            @block.scalar
            def _(act):
                dve_t.wait(act, "centre")
                act_t.did("sq", act.activation(c2, y, ACT.Square))
                dve_t.wait(act, "var")
                act_t.did("sqrt", act.activation(rs, rs, ACT.Sqrt))
                dve_t.wait(act, "norm")
                act_t.did("affine", act.activation(y, y, ACT.Identity, bias=pp("ln_b"), scale=pp("ln_w")))

            @block.sync
            def _(sp):
                dve_t.wait(sp, "gate")
                sp.dma_start(md[bass.ds(p + NP, 1), :, :].rearrange("a p t -> p (a t)"), y).then_inc(y_out, 16)
                sp.wait_ge(y_out, 16)


def rwkv(nc, io, sb, zd, md):
    with ExitStack() as ctx:
        rw = Rwkv(nc, ctx)
        nd = nc.dram_tensor("n_dram", [4 * NCH, 2, 32, 32], F32).ap()
        wd = nc.dram_tensor("w_dram", [4 * NCH, 2, 32, 32], F32).ap()
        rw_setup(nc, io, sb, rw, zd)
        with nc.Fori(0, NP) as p:
            rw_features(nc, io, sb, rw, zd, p)
            rw_grams(nc, io, sb, rw)
            rw_invert(nc, io, sb, rw, nd, wd)
            rw_solve(nc, sb, rw)
            rw_scan(nc, io, sb, rw, p)
            rw_finish(nc, sb, rw, md, p)


def mixer(nc, io, sb, zd, md):
    with nc.sbuf_tensor("mx_u", [P, NP, T], F32) as u:
        with nc.sbuf_tensor("h1_hi", [P, KD, T], F32R) as h_hi, nc.sbuf_tensor("h1_lo", [P, KD, T], F32R) as h_lo:
            norm_stage(nc, sb, 1, h_hi, h_lo)
            project_stage(nc, io, sb, h_hi, h_lo, zd, u)
        fourier_stage(nc, io, sb, u, md)


def out_stage(nc, io, sb, y):
    with Stage(nc) as st, nc.psum_tensor("ou_ps", [P, 8, 512], F32) as ps, nc.sbuf_tensor("ou_y", [P, 4, D], F32) as rows:
        turned, stored = st.sem("turned"), [st.sem(f"stored{n}") for n in range(4)]
        copied = {0: st.sem("copied_dve"), 1: st.sem("copied_act")}
        with st.block() as block:
            @block.tensor
            def _(pe):
                for n in range(2 * NT):
                    t, half = n // 2, n % 2
                    if n >= 8:
                        pe.wait_ge(copied[n % 2], (n - 8) // 2 + 1)
                    for k in range(4):
                        last = pe.transpose(ps[:, n % 8, k * P:(k + 1) * P], y[:, half * 4 + k, t * P:(t + 1) * P],
                                            sb["cst"][:, C_ID:C_ID + P])
                    last.then_inc(turned, 1)

            def copy(eng, half, do):
                for t in range(NT):
                    eng.wait_ge(turned, 2 * t + half + 1)
                    if t >= 4:
                        eng.wait_ge(stored[t % 4], 16 * (t // 4))
                    do(rows[:, t % 4, half * 512:(half + 1) * 512], ps[:, (2 * t + half) % 8, :]).then_inc(copied[half], 1)

            @block.vector
            def _(dve):
                copy(dve, 0, dve.tensor_copy)

            @block.scalar
            def _(act):
                copy(act, 1, lambda o, i: act.activation(o, i, ACT.Copy))

            @block.sync
            def _(sp):
                for t in range(NT):
                    sp.wait_ge(copied[0], t + 1)
                    sp.wait_ge(copied[1], t + 1)
                    dst = io["y_sample"][0, t * P:(t + 1) * P, :] if t * P < TS else io["y_prompt"][0, :, :]
                    sp.dma_start(dst, rows[:, t % 4, :]).then_inc(stored[t % 4], 16)
                for n in range(4):
                    sp.wait_ge(stored[n], 16 * len(range(n, NT, 4)))


def program(nc, io, upto=99):
    with ExitStack() as ctx:
        def keep(name, shape, dt=F32):
            return ctx.enter_context(nc.sbuf_tensor(name, shape, dt))

        sb = {"cst": keep("cst", [P, NCST]), "prm": keep("prm", [P, NPRM]), "mod": keep("mod", [P, NMOD * KD, 2]),
              "bmod": keep("bmod", [P, NMOD * KD])}
        zd = nc.dram_tensor("z_dram", [NZ, P, T], F32).ap()
        md = nc.dram_tensor("mixed_dram", [KD, P, T], F32).ap()
        xd = nc.dram_tensor("x_dram", [KD, P, T], F32).ap()
        with nc.sbuf_tensor("x", [P, KD, T], F32) as x:
            sb["x"] = x
            load_stage(nc, io, sb)
            mod_stage(nc, io, sb)
            with nc.sbuf_tensor("h0_hi", [P, KD, T], F32R) as h_hi, nc.sbuf_tensor("h0_lo", [P, KD, T], F32R) as h_lo:
                norm_stage(nc, sb, 0, h_hi, h_lo)
                ffn_stage(nc, io, sb, 0, h_hi, h_lo)
            mixer(nc, io, sb, zd, md)
            spill(nc, x, xd, False)
        rwkv(nc, io, sb, zd, md)
        with nc.sbuf_tensor("x_again", [P, KD, T], F32) as x:
            sb["x"] = x
            spill(nc, x, xd, True)
            output_stage(nc, io, sb, md)
            if upto >= 3:
                with nc.sbuf_tensor("h2_hi", [P, KD, T], F32R) as h_hi, nc.sbuf_tensor("h2_lo", [P, KD, T], F32R) as h_lo:
                    norm_stage(nc, sb, 2, h_hi, h_lo)
                    ffn_stage(nc, io, sb, 1, h_hi, h_lo)
            with nc.sbuf_tensor("y", [P, KD, T], F32) as y:
                if upto >= 3:
                    norm_stage(nc, sb, 3, y, None)
                out_stage(nc, io, sb, y if upto >= 3 else x)


OUTPUTS = (("y_prompt", (1, TP, D)), ("y_sample", (1, TS, D)), ("state_f", (1, 1, 2 * NP, HS, HS)),
           ("state_b", (1, 1, 2 * NP, HS, HS)))


def kernel(**inputs):
    import concourse.bacc as bacc
    from concourse.bass_utils import run_bass_kernel_spmd

    nc = bacc.Bacc("TRN2", target_bir_lowering=False, num_devices=1)
    arrays = {name: np.ascontiguousarray(a) for name, a in inputs.items()}
    for name, a in zip(("consts", "feat", "dft_s", "dft_p"), constants()):
        arrays[name] = np.ascontiguousarray(a)
    io = {name: nc.dram_tensor(name, a.shape, mybir.dt.from_np(a.dtype), kind="ExternalInput").ap()
          for name, a in arrays.items()}
    for name, shape in OUTPUTS:
        io[name] = nc.dram_tensor(name, shape, F32, kind="ExternalOutput").ap()
    program(nc, io)
    result = run_bass_kernel_spmd(nc, [arrays], core_ids=[0]).results[0]
    return tuple(result[name] for name, _ in OUTPUTS)
```

```python
from contextlib import ExitStack
from itertools import count

import numpy as np

import concourse.bass as bass
from concourse import mybir

ALU = mybir.AluOpType
ACT = mybir.ActivationFunctionType
F32 = mybir.dt.float32
F32R = mybir.dt.float32r
BF16 = mybir.dt.bfloat16

P = 128
D = 1024
KD = D // P
TS = 1024
TP = 128
T = TS + TP
NT = T // P
NC = 3
CW = T // NC
STREAMS = ((0, TS), (TS, T))
GRID_W = 64
FF = 2816
GROUPS = FF // P // 2
NMOD = 9
DH = 512
NP = DH // P
HS = 64
NCH = T // HS
SCH = TS // HS
NZ = 15
DECAY = float(np.exp(-0.5))
RMS_EPS = 1e-6
GN_EPS = 64e-5

PRM = {}
for _name, _n in (("c", 8), ("c_ctx", 8), ("norm_g", 24), ("final_norm", 8), ("shift_mu", 15), ("w0", 8), ("a0", 8),
                  ("k_k", 4), ("k_a", 4), ("r_k", 4), ("ln_w", 4), ("ln_b", 4)):
    PRM[_name] = sum(n for _, n in PRM.values()), _n
NPRM = sum(n for _, n in PRM.values())

C_ID, C_MASK, C_ONE, C_BLK, C_CLS = 0, 128, 384, 512, 640
NCST = 644


def constants():
    c = np.zeros((P, NCST), np.float32)
    c[:, C_ID:C_ID + P] = np.eye(P)
    s, t = np.arange(P)[:, None] % HS, np.arange(HS)[None, :]
    c[:, C_MASK:C_MASK + 256] = np.concatenate([s < t, s <= t, s > t, s >= t], 1)
    c[:, C_ONE:C_ONE + P] = 1.0 / D
    c[:, C_BLK:C_BLK + P] = np.kron(np.eye(2), np.ones((HS, HS)))
    c[:, C_CLS:C_CLS + 4] = np.arange(P)[:, None] % 4 == np.arange(4)[None, :]
    f = np.arange(HS)
    ang = 2 * np.pi * ((f[:, None] * f[None, :]) % HS) / HS
    feat = np.stack([np.concatenate([np.kron(np.eye(2), np.cos(ang)), np.kron(np.eye(2), -np.sin(ang))], 1)
                     / np.sqrt(n * HS) for n in (TS, TP)], 1)
    tabs = []
    for n, m in ((TS, TS // 2), (TP, TP)):
        i = np.arange(m, dtype=np.int64)
        a = 2 * np.pi * ((i[:, None] * i[None, :]) % n) / n
        tabs.append(np.stack([np.cos(a), np.sin(a)], 1).astype(np.float32))
    alternate = (-1.0) ** (np.arange(P)[:, None] + np.arange(TS // 2)[None, :])
    return c, feat.astype(np.float32), tabs[0], tabs[1], alternate.astype(np.float32)


def fresh(name, count=count()):
    return f"{name}{next(count)}"


class Steps:

    def __init__(self, sem, names):
        self.sem, self.names, self.n = sem, list(names), 0
        self.count = {name: i + 1 for i, name in enumerate(self.names)}
        assert len(self.count) == len(self.names)

    def did(self, name, ins):
        assert self.names[self.n] == name, (self.names[self.n], name)
        self.n += 1
        ins.then_inc(self.sem, 1)

    def wait(self, eng, name):
        eng.wait_ge(self.sem, self.count[name])


class Stage:

    def __init__(self, nc):
        self.nc, self.sems, self.ctx = nc, [], ExitStack()

    def sem(self, name):
        s = self.ctx.enter_context(self.nc.semaphore(name))
        self.sems.append(s)
        return s

    def __enter__(self):
        self.ctx.__enter__()
        return self

    def block(self):
        return self.nc.Block()

    def __exit__(self, *a):
        if a[0] is None:
            with self.nc.Block() as block:
                @block.sync
                def _(sp):
                    for s in self.sems:
                        sp.sem_clear(s)
        return self.ctx.__exit__(*a)


def mm3(pe, out, w_hi, w_lo, x_hi, x_lo, start, stop):
    pe.matmul(out, w_lo, x_hi, start=start, stop=False)
    pe.matmul(out, w_hi, x_lo, start=False, stop=False)
    return pe.matmul(out, w_hi, x_hi, start=False, stop=stop)


def parts(c):
    out = []
    for s, (a, b) in enumerate(STREAMS):
        lo, hi = max(a, c * CW), min(b, (c + 1) * CW)
        if lo < hi:
            out.append((s, lo - c * CW, hi - c * CW))
    return out


def load_stage(nc, io, sb):
    with Stage(nc) as st, nc.psum_tensor("ld_ps", [P, 8, 512], F32) as ps, \
            nc.sbuf_tensor("ld_x", [P, NT, D], F32) as xin, nc.sbuf_tensor("ld_p", [P, 2, P], F32) as prow:
        consts_in, rows_in = st.sem("consts_in"), st.sem("rows_in")
        x_in = [st.sem(f"x_in{t}") for t in range(NT)]
        pe_s, dve_s, act_s = st.sem("pe_s"), st.sem("dve_s"), st.sem("act_s")
        pe_t = Steps(pe_s, ["prm", "bias"] + [f"x{n}" for n in range(2 * NT)])
        dve_t = Steps(dve_s, ["prm", "bias"] + [f"x{n}" for n in range(0, 2 * NT, 2)])
        act_t = Steps(act_s, [f"x{n}" for n in range(1, 2 * NT, 2)])
        rows = [(io["c"], "c"), (io["c_ctx"].rearrange("(a n) -> a n", a=1), "c_ctx"),
                (io["norm_g"].rearrange("l i n -> (l i) n"), "norm_g"),
                (io["final_norm"].rearrange("(a n) -> a n", a=1), "final_norm"), (io["shift_mu"], "shift_mu"),
                (io["decay_w0"].rearrange("l i n -> (l i) n"), "w0"), (io["iclr_a0"].rearrange("l i n -> (l i) n"), "a0"),
                (io["k_k"], "k_k"), (io["k_a"], "k_a"), (io["r_k"], "r_k"), (io["ln_x_w"], "ln_w"), (io["ln_x_b"], "ln_b")]
        with st.block() as block:
            @block.sync
            def _(sp):
                sp.dma_start(sb["cst"][:, :], io["consts"]).then_inc(consts_in, 16)
                for t in range(0, NT):
                    src = io["x_sample"][0, t * P:(t + 1) * P, :] if t * P < TS else io["x_prompt"][0, :, :]
                    sp.dma_start(xin[:, t, :], src).then_inc(x_in[t], 16)

            @block.scalar
            def _(act):
                for src, name in rows:
                    at, n = PRM[name]
                    act.dma_start(prow[at:at + n, 0, :], src.rearrange("i (k p) -> (i k) p", p=P)).then_inc(rows_in, 16)
                act.dma_start(prow[0:NMOD * KD, 1, :], io["b_mod"].rearrange("i (k p) -> (i k) p", p=P))\
                   .then_inc(rows_in, 16)
                for n in range(1, 2 * NT, 2):
                    t, half = n // 2, n % 2
                    pe_t.wait(act, f"x{n}")
                    act_t.did(f"x{n}", act.activation(
                        sb["x"][:, half * 4:half * 4 + 4, t * P:(t + 1) * P],
                        ps[:, n % 6, :].rearrange("p (k t) -> p k t", k=4), ACT.Copy))

            @block.tensor
            def _(pe):
                pe.wait_ge(consts_in, 16)
                pe.wait_ge(rows_in, 16 * (len(rows) + 1))
                ident = sb["cst"][:, C_ID:C_ID + P]
                pe_t.did("prm", pe.transpose(ps[:, 6, 0:NPRM], prow[0:NPRM, 0, :], ident[0:NPRM, 0:NPRM]))
                nb = NMOD * KD
                pe_t.did("bias", pe.transpose(ps[:, 7, 0:nb], prow[0:nb, 1, :], ident[0:nb, 0:nb]))
                for n in range(2 * NT):
                    t, half = n // 2, n % 2
                    if half == 0:
                        pe.wait_ge(x_in[t], 16)
                    if n >= 6:
                        (dve_t if n % 2 == 0 else act_t).wait(pe, f"x{n - 6}")
                    for k in range(4):
                        last = pe.transpose(ps[:, n % 6, k * P:(k + 1) * P],
                                            xin[:, t, (half * 4 + k) * P:(half * 4 + k + 1) * P], ident)
                    pe_t.did(f"x{n}", last)

            @block.vector
            def _(dve):
                pe_t.wait(dve, "prm")
                dve_t.did("prm", dve.tensor_copy(sb["prm"][:, :], ps[:, 6, 0:NPRM]))
                pe_t.wait(dve, "bias")
                dve_t.did("bias", dve.tensor_copy(sb["bmod"][:, :], ps[:, 7, 0:NMOD * KD]))
                for n in range(0, 2 * NT, 2):
                    t, half = n // 2, n % 2
                    pe_t.wait(dve, f"x{n}")
                    dve_t.did(f"x{n}", dve.tensor_copy(
                        sb["x"][:, half * 4:half * 4 + 4, t * P:(t + 1) * P],
                        ps[:, n % 6, :].rearrange("p (k t) -> p k t", k=4)))


def mod_stage(nc, io, sb):
    SLOTS = 3
    with Stage(nc) as st, nc.psum_tensor("md_ps", [P, 4, 512], F32) as ps, \
            nc.sbuf_tensor("md_w", [P, SLOTS, KD, D], F32) as w, nc.sbuf_tensor("md_c", [P, KD, 32], F32) as cpad, \
            nc.sbuf_tensor("md_sum", [P, 2, 512], F32) as sums, nc.sbuf_tensor("md_q", [P, 2, 16], F32) as quad:
        w_in = [st.sem(f"w_in{n}") for n in range(SLOTS)]
        c_zero, c_ready, summed, copied = st.sem("c_zero"), st.sem("c_ready"), st.sem("summed"), st.sem("copied")
        turned, quad_copied, own, done = st.sem("turned"), st.sem("quad_copied"), st.sem("own"), st.sem("done")
        wsrc = io["w_mod"].rearrange("l (k p) n -> p (l k) n", p=P)
        with st.block() as block:
            @block.sync
            def _(sp):
                for j in range(SLOTS):
                    sp.dma_start(w[:, j, :, :], wsrc[:, :, j * D:(j + 1) * D]).then_inc(w_in[j], 16)
                with sp.Fori(0, NMOD // SLOTS - 1) as i:
                    for j in range(SLOTS):
                        sp.wait_ge(summed, i * SLOTS + (j + 1))
                        sp.dma_start(w[:, j, :, :], wsrc[:, :, bass.ds(i * (SLOTS * D) + (SLOTS + j) * D, D)])\
                          .then_inc(w_in[j], 16)

            @block.gpsimd
            def _(pool):
                pool.memset(cpad[:, :, :], 0.0).then_inc(c_zero, 1)

            @block.scalar
            def _(act):
                act.wait_ge(c_zero, 1)
                for s, name in enumerate(("c", "c_ctx")):
                    at, n = PRM[name]
                    act.activation(cpad[:, :, s:s + 1], sb["prm"][:, at:at + n].unsqueeze(2), ACT.Silu)\
                       .then_inc(c_ready, 1)

            @block.tensor
            def _(pe):
                pe.wait_ge(c_ready, 2)
                ident = sb["cst"][:, C_ID:C_ID + P]
                with pe.Fori(0, NMOD // SLOTS) as i:
                    for j in range(SLOTS):
                        pe.wait_ge(w_in[j], i * 16 + 16)
                        for kk in range(KD // 2):
                            for g in range(4):
                                n, k = g // 2, g % 2 * (KD // 2) + kk
                                last = pe.matmul(ps[32 * g:32 * g + 32, 0, :], cpad[:, k, :],
                                                 w[:, j, k, n * 512:(n + 1) * 512], start=kk == 0, stop=kk == KD // 2 - 1)
                        last.then_inc(summed, 1)
                        pe.wait_ge(copied, i * SLOTS + (j + 1))
                        pe.wait_ge(quad_copied, i * SLOTS + (j + 1))
                        for cc in range(4):
                            last = pe.transpose(ps[:, 1, cc * P:(cc + 1) * P], sums[:, 0, cc * P:(cc + 1) * P], ident)
                        last.then_inc(turned, 1)

            @block.vector
            def _(dve):
                dve.sem_inc(quad_copied, 1)
                with dve.Fori(0, NMOD // SLOTS) as i:
                    for j in range(SLOTS):
                        dve.wait_ge(summed, i * SLOTS + (j + 1))
                        dve.tensor_copy(sums[:, 0, :], ps[:, 0, :]).then_inc(copied, 1)
                        dve.wait_ge(turned, i * SLOTS + (j + 1))
                        for n in range(2):
                            for kh in range(2):
                                c0 = 64 * n + 32 * kh
                                last = dve.tensor_copy(
                                    quad[:, kh, 8 * n:8 * n + 8].rearrange("p (c s) -> p c s", s=2),
                                    ps[:, 1, :].rearrange("p (c q) -> p c q", q=P)[:, :, c0:c0 + 2])
                                last.then_inc(own, 1)
                        dve.wait_ge(own, i * (4 * SLOTS) + 4 * (j + 1))
                        dve.tensor_tensor(sb["mod"][:, bass.ds(i * (SLOTS * KD) + j * KD, KD), :],
                                          quad[:, 0, :].rearrange("p (c s) -> p c s", s=2),
                                          quad[:, 1, :].rearrange("p (c s) -> p c s", s=2), ALU.add)\
                           .then_inc(quad_copied, 1)
                        dve.wait_ge(quad_copied, i * SLOTS + (j + 2))
                mod = sb["mod"]
                steps = Steps(done, ["bias", "sc", "g", "h0", "h2"])
                steps.did("bias", dve.tensor_tensor(mod[:, :, :], mod[:, :, :],
                                                    sb["bmod"][:, :].unsqueeze(2).to_broadcast([P, NMOD * KD, 2]), ALU.add))
                steps.wait(dve, "bias")
                mv = mod[:, :, :].rearrange("p (i m k) s -> p i m (k s)", i=3, m=3)
                at, n = PRM["norm_g"]
                steps.did("sc", dve.tensor_scalar(mv[:, :, 1, :], mv[:, :, 1, :], 1.0, None, ALU.add))
                steps.wait(dve, "sc")
                for i in range(3):
                    m = mod[:, (3 * i + 1) * KD:(3 * i + 2) * KD, :]
                    last = dve.tensor_tensor(m, m, sb["prm"][:, at + i * KD:at + (i + 1) * KD].unsqueeze(2)
                                             .to_broadcast([P, KD, 2]), ALU.mult)
                steps.did("g", last)
                steps.did("h0", dve.tensor_scalar(mv[:, 0, 2, :], mv[:, 0, 2, :], 0.5, None, ALU.mult))
                steps.did("h2", dve.tensor_scalar(mv[:, 2, 2, :], mv[:, 2, 2, :], 0.5, None, ALU.mult))


class Norm:

    def __init__(self, st, sb, i, h_hi, h_lo, tmp, inv, ps, stats, banks):
        self.sb, self.i, self.h_hi, self.h_lo, self.inv, self.ps, self.stats, self.banks = \
            sb, i, h_hi, h_lo, inv, ps, stats, banks
        self.sq, self.nrm, self.acc = tmp
        self.final = h_lo is None
        self.pe_t = Steps(st.sem("norm_pe"), [f"{n}{c}" for c in range(NC) for n in ("sum", "wide")])
        self.act_t = Steps(st.sem("norm_act"), [
            *self.names("sq", 0, 0, KD), *self.names("sq", 1, 0, KD // 2), "sqrt0", *self.names("sq", 1, KD // 2, KD),
            *self.hi(0, 0, 3), "sqrt1", *self.hi(0, 3, KD),
            *[x for k in range(4) for x in (*self.names("sq", 2, 2 * k, 2 * k + 2), *self.hi(1, k, k + 1))],
            *self.hi(1, 4, 6), "sqrt2", *self.hi(1, 6, KD), *self.hi(2, 0, KD)])
        self.dve_t = Steps(st.sem("norm_dve"), [
            *self.names("acc", 0, 1, KD), *self.names("acc", 1, 1, KD // 2), "ms0", *self.names("acc", 1, KD // 2, KD),
            "inv0", "wide0", *self.chunk(0, 0, 2), "ms1", *self.chunk(0, 2, 4), "inv1", *self.chunk(0, 4, 5), "wide1",
            *self.chunk(0, 5, KD + 1),
            *[x for k in range(4) for x in (*self.names("acc", 2, max(1, 2 * k), 2 * k + 2), *self.chunk(1, k, k + 1))],
            *self.chunk(1, 4, 6), "ms2", *self.chunk(1, 6, 7), "inv2", *self.chunk(1, 7, 8), "wide2",
            *self.chunk(1, 8, KD + 1), *self.chunk(2, 0, KD + 1)])

    @staticmethod
    def names(name, c, first, last):
        return [f"{name}{c}_{k}" for k in range(first, last)]

    def hi(self, c, first, last):
        return [] if self.final else self.names("hi", c, first, last)

    def chunk(self, c, first, last):
        out = []
        for k in range(first, last):
            out += [f"n{c}_{k}"] * (k < KD) + [f"lo{c}_{k - 1}"] * (k > 0 and not self.final)
        return out

    def scale(self, k, s):
        if self.final:
            at = PRM["final_norm"][0] + k
            return self.sb["prm"][:, at:at + 1]
        return self.sb["mod"][:, (3 * self.i + 1) * KD + k, s:s + 1]

    def shift(self, k, s):
        return self.sb["mod"][:, 3 * self.i * KD + k, s:s + 1]

    def ready(self, eng, c):
        self.dve_t.wait(eng, f"n{c}_{KD - 1}" if self.final else f"lo{c}_{KD - 1}")

    def temp(self, t, c, k):
        n = (c * KD + k) % 3
        return t[:, n * CW:(n + 1) * CW]

    def pe(self, pe, c):
        for c in ((0, 1), (2, ), ())[c]:
            self.dve_t.wait(pe, f"acc{c}_{KD - 1}")
            for t in range(NC):
                last = pe.matmul(self.ps[:, self.stats, c * NC + t:c * NC + t + 1],
                                 self.acc[:, (c * NC + t) * P:(c * NC + t + 1) * P],
                                 self.sb["cst"][:, C_ONE:C_ONE + 1], start=True, stop=True)
            self.pe_t.did(f"sum{c}", last)
            self.dve_t.wait(pe, f"wide{c}")
            for t in range(NC):
                at = (c * NC + t) * P
                last = pe.matmul(self.ps[:, self.banks[c], t * P:(t + 1) * P], self.acc[:, at:at + P],
                                 self.sb["cst"][:, C_ID:C_ID + P], start=True, stop=True)
            self.pe_t.did(f"wide{c}", last)

    def act_squares(self, act, c, first, last):
        for k in range(first, last):
            if c or k >= 3:
                n, kk = divmod(c * KD + k - 3, KD)
                self.dve_t.wait(act, f"acc{n}_{max(kk, 1)}")
            self.act_t.did(f"sq{c}_{k}", act.activation(self.temp(self.sq, c, k), self.sb["x"][:, k, c * CW:(c + 1) * CW],
                                                        ACT.Square))

    def act_sqrt(self, act, c):
        self.dve_t.wait(act, f"ms{c}")
        inv = self.inv[:, c * NC:(c + 1) * NC]
        self.act_t.did(f"sqrt{c}", act.activation(inv, inv, ACT.Sqrt))

    def act_head(self, act):
        self.act_squares(act, 0, 0, KD)
        self.act_squares(act, 1, 0, KD // 2)
        self.act_sqrt(act, 0)
        self.act_squares(act, 1, KD // 2, KD)

    def act_chunk(self, act, c):
        for k in range(KD):
            if c == 0 and k == 3:
                self.act_sqrt(act, 1)
            if c == 1 and k < 4:
                self.act_squares(act, 2, 2 * k, 2 * k + 2)
            if c == 1 and k == 6:
                self.act_sqrt(act, 2)
            if self.final:
                continue
            self.dve_t.wait(act, f"n{c}_{k}")
            for s, a, b in parts(c):
                last = act.activation(self.h_hi[:, k, c * CW + a:c * CW + b], self.temp(self.nrm, c, k)[:, a:b],
                                      ACT.Identity, bias=self.shift(k, s))
            self.act_t.did(f"hi{c}_{k}", last)

    def dve_sums(self, dve, c, first, last):
        acc = self.acc[:, c * CW:(c + 1) * CW]
        for k in range(max(first, 1), last):
            self.act_t.wait(dve, f"sq{c}_{k}")
            if k > 1:
                self.dve_t.wait(dve, f"acc{c}_{k - 1}")
            self.dve_t.did(f"acc{c}_{k}", dve.tensor_tensor(acc, self.temp(self.sq, c, 0) if k == 1 else acc,
                                                            self.temp(self.sq, c, k), ALU.add))

    def dve_mean(self, dve, c):
        self.pe_t.wait(dve, f"sum{c}")
        cols = slice(c * NC, (c + 1) * NC)
        self.dve_t.did(f"ms{c}", dve.tensor_scalar(self.inv[:, cols], self.ps[:, self.stats, cols], RMS_EPS, None, ALU.add))

    def dve_inverse(self, dve, c):
        self.act_t.wait(dve, f"sqrt{c}")
        inv = self.inv[:, c * NC:(c + 1) * NC]
        self.dve_t.did(f"inv{c}", dve.reciprocal(inv, inv))

    def dve_widen(self, dve, c):
        self.dve_t.wait(dve, f"inv{c}")
        self.dve_t.did(f"wide{c}", dve.tensor_copy(
            self.acc[:, c * CW:(c + 1) * CW].rearrange("p (t n) -> p t n", t=NC),
            self.inv[:, c * NC:(c + 1) * NC].unsqueeze(2).to_broadcast([P, NC, P])))

    def dve_head(self, dve):
        self.dve_sums(dve, 0, 1, KD)
        self.dve_sums(dve, 1, 1, KD // 2)
        self.dve_mean(dve, 0)
        self.dve_sums(dve, 1, KD // 2, KD)
        self.dve_inverse(dve, 0)
        self.dve_widen(dve, 0)

    def dve_chunk(self, dve, c):
        def lower(k):
            self.act_t.wait(dve, f"hi{c}_{k}")
            for s, a, b in parts(c):
                cols = slice(c * CW + a, c * CW + b)
                last = dve.scalar_tensor_tensor(self.h_lo[:, k, cols], self.temp(self.nrm, c, k)[:, a:b],
                                                self.shift(k, s), self.h_hi[:, k, cols].bitcast(F32), ALU.add, ALU.subtract)
            self.dve_t.did(f"lo{c}_{k}", last)

        rstd, x = self.ps[:, self.banks[c], 0:CW], self.sb["x"]
        extra = {(0, 2): (self.dve_mean, 1), (0, 4): (self.dve_inverse, 1), (0, 5): (self.dve_widen, 1),
                 (1, 6): (self.dve_mean, 2), (1, 7): (self.dve_inverse, 2), (1, 8): (self.dve_widen, 2)}
        for k in range(KD + 1):
            if (c, k) in extra:
                what, n = extra[c, k]
                what(dve, n)
            if c == 1 and k < 4:
                self.dve_sums(dve, 2, 2 * k, 2 * k + 2)
            if k == KD:
                if not self.final:
                    lower(KD - 1)
                continue
            if k == 0:
                self.pe_t.wait(dve, f"wide{c}")
            if self.final:
                cols = slice(c * CW, (c + 1) * CW)
                self.dve_t.did(f"n{c}_{k}", dve.scalar_tensor_tensor(self.h_hi[:, k, cols], x[:, k, cols], self.scale(k, 0),
                                                                     rstd, ALU.mult, ALU.mult))
                continue
            if c * KD + k >= 3:
                self.dve_t.wait(dve, "lo{}_{}".format(*divmod(c * KD + k - 3, KD)))
            for s, a, b in parts(c):
                last = dve.scalar_tensor_tensor(self.temp(self.nrm, c, k)[:, a:b], x[:, k, c * CW + a:c * CW + b],
                                                self.scale(k, s), rstd[:, a:b], ALU.mult, ALU.mult)
            self.dve_t.did(f"n{c}_{k}", last)
            if k:
                lower(k - 1)


def ffn_stage(nc, io, sb, f, h_hi, h_lo):
    UNITS, RAW = 6, 3
    G0, U0, G1, U1, D0, D1 = range(UNITS)
    x = sb["x"]
    with Stage(nc) as st, nc.psum_tensor(f"ff_ps{f}", [P, 8, 512], F32) as ps, \
            nc.sbuf_tensor(f"ff_raw{f}", [P, RAW, D], F32) as raw, nc.sbuf_tensor(f"ff_whi{f}", [P, UNITS, D], F32R) as w_hi, \
            nc.sbuf_tensor(f"ff_wlo{f}", [P, UNITS, D], F32R) as w_lo, \
            nc.sbuf_tensor(f"ff_s{f}", [P, 4, CW], F32) as buf, nc.sbuf_tensor(f"ff_n{f}", [P, 2, T], F32) as tmp, \
            nc.sbuf_tensor(f"ff_uhi{f}", [P, 2, T], F32R) as hid_hi, nc.sbuf_tensor(f"ff_ulo{f}", [P, 2, T], F32R) as hid_lo, \
            nc.sbuf_tensor(f"ff_inv{f}", [P, NT], F32) as inv:
        silu, hid = buf[:, 0:2, :], buf[:, 2:4, :]
        norm = Norm(st, sb, 2 * f, h_hi, h_lo,
                    [tmp[:, 0, :], buf[:, :, :].rearrange("p n c -> p (n c)")[:, 0:T], tmp[:, 1, :]], inv, ps, 4,
                    (5, 6, 7))
        raw_in = [st.sem(f"raw_in{n}") for n in range(RAW)]
        w_hi_s, w_lo_s = st.sem("w_hi_s"), st.sem("w_lo_s")
        gate_done, up_done, down_done = st.sem("gate_done"), st.sem("up_done"), st.sem("down_done")
        gate_free, up_free, down_free = st.sem("gate_free"), st.sem("up_free"), st.sem("down_free")
        hid_hi_s, hid_lo_s = st.sem("hid_hi_s"), st.sem("hid_lo_s")
        TILES, DOWNS = 2 * NC, NC * KD

        def unit_src(g, u):
            if u in (D0, D1):
                return io["ffn_w_down"][0, f, bass.ds((g * 2 + (u - D0)) * P, P), :]
            src = io["ffn_w_gate"] if u in (G0, G1) else io["ffn_w_up"]
            m = u // 2
            return src[0, f].rearrange("(k p) n -> p k n", p=P)[:, :, bass.ds((g * 2 + m) * P, P)]

        def unit_dst(t, u, slot):
            return t[:, slot, :] if u in (D0, D1) else t[:, slot, :].rearrange("p (k n) -> p k n", k=KD)

        with st.block() as block:
            @block.sync
            def _(sp):
                for u in range(RAW):
                    sp.dma_start(unit_dst(raw, u, u), unit_src(0, u)).then_inc(raw_in[u], 16)

                def rest(g):
                    for u in range(RAW, UNITS):
                        sp.wait_ge(w_lo_s, g * UNITS + (u - RAW + 1))
                        sp.dma_start(unit_dst(raw, u, u % RAW), unit_src(g, u)).then_inc(raw_in[u % RAW], 16)

                with sp.Fori(0, GROUPS - 1) as g:
                    rest(g)
                    for u in range(RAW):
                        sp.wait_ge(w_lo_s, g * UNITS + (u + RAW + 1))
                        sp.dma_start(unit_dst(raw, u, u), unit_src(g + 1, u)).then_inc(raw_in[u], 16)
                rest(GROUPS - 1)

            @block.tensor
            def _(pe):
                def group(g, first):
                    for t in range(TILES):
                        m, c = t // NC, t % NC
                        cols = slice(c * CW, (c + 1) * CW)
                        if first and m == 0:
                            norm.pe(pe, c)
                            norm.ready(pe, c)
                        for which, base, free, done in ((G0, 0, gate_free, gate_done), (U0, 2, up_free, up_done)):
                            u = which + 2 * m
                            if c == 0:
                                pe.wait_ge(w_lo_s, g * UNITS + (u + 1))
                            pe.wait_ge(free, g * TILES + (t + 1))
                            for k in range(KD):
                                ks = slice(k * P, (k + 1) * P)
                                last = mm3(pe, ps[:, base + t % 2, 0:CW], w_hi[:, u, ks], w_lo[:, u, ks],
                                           h_hi[:, k, cols], h_lo[:, k, cols], k == 0, k == KD - 1)
                            last.then_inc(done, 1)
                    for n in range(DOWNS):
                        c, o = n // KD, n % KD
                        if n == 0:
                            pe.wait_ge(w_lo_s, g * UNITS + UNITS)
                        if o == 0:
                            pe.wait_ge(hid_lo_s, g * TILES + (NC + c + 1))
                        pe.wait_ge(down_free, g * DOWNS + (n + 1))
                        for m in range(2):
                            os = slice(o * P, (o + 1) * P)
                            cols = slice(c * CW, (c + 1) * CW)
                            last = mm3(pe, ps[:, 4 + n % 4, 0:CW], w_hi[:, D0 + m, os], w_lo[:, D0 + m, os],
                                       hid_hi[:, m, cols], hid_lo[:, m, cols], m == 0, m == 1)
                        last.then_inc(down_done, 1)
                group(0, True)
                with pe.Fori(1, GROUPS) as g:
                    group(g, False)

            @block.scalar
            def _(act):
                act.sem_inc(gate_free, 2)

                def split(g, u):
                    act.wait_ge(raw_in[u % RAW], (g * 2 + (u // RAW + 1)) * 16)
                    act.activation(w_hi[:, u, :], raw[:, u % RAW, :], ACT.Copy).then_inc(w_hi_s, 1)

                def hidden(g, t):
                    act.wait_ge(gate_done, g * TILES + (t + 1))
                    act.wait_ge(up_free, g * TILES + (t + 1))
                    act.activation(silu[:, t % 2, :], ps[:, t % 2, 0:CW], ACT.Silu).then_inc(gate_free, 1)
                    m, c = t // NC, t % NC
                    act.wait_ge(up_free, g * TILES + (t + 3))
                    act.wait_ge(down_free, g * DOWNS + 4)
                    act.activation(hid_hi[:, m, c * CW:(c + 1) * CW], hid[:, t % 2, :], ACT.Copy).then_inc(hid_hi_s, 1)

                def group(g, last):
                    for t in range(TILES):
                        hidden(g, t)
                        if t == NC - 1:
                            act.wait_ge(up_done, g * TILES + NC)
                            split(g, D0)
                            split(g, D1)
                        if t == NC + 1 and not last:
                            split(g + 1, G0)
                            split(g + 1, U0)
                    if not last:
                        act.wait_ge(up_done, g * TILES + TILES)
                        split(g + 1, G1)
                        split(g + 1, U1)

                norm.act_head(act)
                split(0, G0)
                norm.act_chunk(act, 0)
                split(0, U0)
                norm.act_chunk(act, 1)
                split(0, G1)
                norm.act_chunk(act, 2)
                split(0, U1)
                with act.Fori(0, GROUPS - 1) as g:
                    group(g, False)
                group(GROUPS - 1, True)

            @block.vector
            def _(dve):
                dve.sem_inc(up_free, 2)

                def split(g, u):
                    dve.wait_ge(w_hi_s, g * UNITS + (u + 1))
                    dve.tensor_tensor(w_lo[:, u, :], raw[:, u % RAW, :], w_hi[:, u, :].bitcast(F32), ALU.subtract)\
                       .then_inc(w_lo_s, 1)

                def hidden(g, t):
                    m, c = t // NC, t % NC
                    dve.wait_ge(gate_free, g * TILES + (t + 3))
                    dve.wait_ge(up_done, g * TILES + (t + 1))
                    dve.tensor_tensor(hid[:, t % 2, :], ps[:, 2 + t % 2, 0:CW], silu[:, t % 2, :], ALU.mult)\
                       .then_inc(up_free, 1)
                    dve.wait_ge(hid_hi_s, g * TILES + (t + 1))
                    dve.tensor_tensor(hid_lo[:, m, c * CW:(c + 1) * CW], hid[:, t % 2, :],
                                      hid_hi[:, m, c * CW:(c + 1) * CW].bitcast(F32), ALU.subtract).then_inc(hid_lo_s, 1)

                def update(g, n):
                    c, o = n // KD, n % KD
                    dve.wait_ge(down_done, g * DOWNS + (n + 1))
                    for s, a, b in parts(c):
                        xs = x[:, o, c * CW + a:c * CW + b]
                        last = dve.scalar_tensor_tensor(xs, ps[:, 4 + n % 4, a:b],
                                                        sb["mod"][:, (3 * (2 * f) + 2) * KD + o, s:s + 1], xs,
                                                        ALU.mult, ALU.add)
                    last.then_inc(down_free, 1)

                def group(g, last):
                    for t in range(TILES):
                        hidden(g, t)
                        if t == NC - 1:
                            split(g, D0)
                            split(g, D1)
                        if t == NC + 1 and not last:
                            split(g + 1, G0)
                            split(g + 1, U0)
                    for n in range(DOWNS):
                        update(g, n)
                        if n in (7, 15) and not last:
                            split(g + 1, G1 if n == 7 else U1)

                norm.dve_head(dve)
                split(0, G0)
                norm.dve_chunk(dve, 0)
                split(0, U0)
                norm.dve_chunk(dve, 1)
                split(0, G1)
                norm.dve_chunk(dve, 2)
                split(0, U1)
                norm.ready(dve, NC - 1)
                dve.sem_inc(down_free, 4)
                with dve.Fori(0, GROUPS - 1) as g:
                    group(g, False)
                group(GROUPS - 1, True)


def project_stage(nc, io, sb, h_hi, h_lo, zd, u):
    RAW = 2
    with Stage(nc) as st, nc.psum_tensor("pj_ps", [P, 8, 512], F32) as ps, \
            nc.sbuf_tensor("pj_raw", [P, RAW, D], F32) as raw, nc.sbuf_tensor("pj_whi", [P, 2, D], F32R) as w_hi, \
            nc.sbuf_tensor("pj_wlo", [P, 2, D], F32R) as w_lo, nc.sbuf_tensor("pj_z", [P, 2, T], F32) as z, \
            nc.sbuf_tensor("pj_zo", [P, 2, T], F32) as zo, nc.sbuf_tensor("pj_mu", [P, NZ, 7], F32) as mu, \
            nc.sbuf_tensor("pj_n", [P, 3, T], F32) as tmp, nc.sbuf_tensor("pj_inv", [P, NT], F32) as inv:
        norm = Norm(st, sb, 1, h_hi, h_lo, [tmp[:, n, :] for n in range(3)], inv, ps, 6, (7, 3, 5))
        raw_in = [st.sem(f"raw_in{n}") for n in range(RAW)]
        z_out = [st.sem(f"z_out{n}") for n in range(2)]
        w_hi_s, w_lo_s, chunk_done, chunk_free = st.sem("w_hi_s"), st.sem("w_lo_s"), st.sem("chunk_done"), st.sem("chunk_free")
        z_copied, shifted, own, mu_s, z_free = st.sem("z_copied"), st.sem("shifted"), st.sem("own"), st.sem("mu_s"), st.sem("z_free")
        wsrc = io["w_in"][0].rearrange("(k p) n -> p k n", p=P)
        NU = NP
        PAIRS, LAST = NZ // 2, NZ - 1
        ADDS = 6
        TILES = NZ + NU

        def load(sp, i, slot):
            col = (i + NU) * P if not isinstance(i, int) or i < NZ else (i - NZ) * P
            sp.dma_start(raw[:, slot, :].rearrange("p (k n) -> p k n", k=KD), wsrc[:, :, bass.ds(col, P)])\
              .then_inc(raw_in[slot], 16)

        with st.block() as block:
            @block.sync
            def _(sp):
                def store(i, b):
                    sp.wait_ge(shifted, i + 1)
                    dst = zd[bass.ds(i, 1), :, :].rearrange("a p t -> p (a t)")
                    sp.dma_start(dst, zo[:, b, :]).then_inc(z_out[b], 16)

                for n in range(4):
                    if n >= 2:
                        sp.wait_ge(w_lo_s, n - 1)
                    load(sp, n, n % 2)
                AHEAD = (NZ - 4) // 2
                with sp.Fori(0, AHEAD) as i:
                    for b in range(2):
                        store(i * 2 + b, b)
                        sp.wait_ge(w_lo_s, i * 2 + (b + 3))
                        load(sp, i * 2 + (b + 4), b)
                for n in range(2 * AHEAD, NZ):
                    store(n, n % 2)
                    if n + 4 < TILES:
                        sp.wait_ge(w_lo_s, n + 3)
                        load(sp, n + 4, n % 2)
                sp.wait_ge(z_out[0], 16 * (PAIRS + 1))
                sp.wait_ge(z_out[1], 16 * PAIRS)

            @block.tensor
            def _(pe):
                def tile(i, b, first=False):
                    for c in range(NC):
                        cols = slice(c * CW, (c + 1) * CW)
                        if first:
                            norm.pe(pe, c)
                            norm.ready(pe, c)
                        if c == 0:
                            pe.wait_ge(w_lo_s, i + 1)
                        pe.wait_ge(chunk_free, i * NC + (c + 1))
                        for k in range(KD):
                            ks = slice(k * P, (k + 1) * P)
                            last = mm3(pe, ps[:, 4 * b + c, 0:CW], w_hi[:, b, ks], w_lo[:, b, ks],
                                       h_hi[:, k, cols], h_lo[:, k, cols], k == 0, k == KD - 1)
                        last.then_inc(chunk_done, 1)
                tile(0, 0, True)
                tile(1, 1)
                with pe.Fori(1, PAIRS) as i:
                    for b in range(2):
                        tile(i * 2 + b, b)
                for n in range(2 * PAIRS, TILES):
                    tile(n, n % 2)

            @block.scalar
            def _(act):
                act.sem_inc(chunk_free, 2 * NC)

                def z_tile(i, b):
                    act.wait_ge(z_free, i + 1)
                    for c in range(NC):
                        act.wait_ge(chunk_done, i * NC + (c + 1))
                        act.activation(z[:, b, c * CW:(c + 1) * CW], ps[:, 4 * b + c, 0:CW], ACT.Copy).then_inc(chunk_free, 1)

                def upper(i, b, count):
                    act.wait_ge(raw_in[b], count)
                    act.activation(w_hi[:, b, :], raw[:, b, :], ACT.Copy).then_inc(w_hi_s, 1)

                norm.act_head(act)
                upper(0, 0, 16)
                norm.act_chunk(act, 0)
                upper(1, 1, 16)
                norm.act_chunk(act, 1)
                norm.act_chunk(act, 2)
                with act.Fori(0, PAIRS) as i:
                    for b in range(2):
                        z_tile(i * 2 + b, b)
                        upper(i * 2 + b + 2, b, (i + 2) * 16)
                for n in range(2 * PAIRS, TILES):
                    if n < NZ:
                        z_tile(n, n % 2)
                    else:
                        for c in range(NC):
                            act.wait_ge(chunk_done, n * NC + c + 1)
                            act.activation(u[:, n - NZ, c * CW:(c + 1) * CW], ps[:, 4 * (n % 2) + c, 0:CW], ACT.Copy)\
                               .then_inc(chunk_free, 1)
                    if n + 2 < TILES:
                        upper(n + 2, n % 2, 16 * ((n + 2) // 2 + 1))

            @block.vector
            def _(dve):
                dve.sem_inc(z_free, 2)
                at, _n = PRM["shift_mu"]
                muv, cls = sb["prm"][:, at:at + NZ], sb["cst"][:, C_CLS:C_CLS + 4]
                mt = Steps(mu_s, ["m0", "m1", "m2", "m3", "one", "up", "down"])
                for j in range(4):
                    mt.did(f"m{j}", dve.tensor_scalar(mu[:, :, j], muv, cls[:, j:j + 1], None, ALU.mult))
                mt.did("one", dve.tensor_scalar(mu[:, :, 6], muv, -1.0, 1.0, ALU.mult, ALU.add))
                mt.wait(dve, "one")
                mt.did("up", dve.tensor_tensor(mu[:, :, 4], mu[:, :, 0], mu[:, :, 2], ALU.add))
                mt.did("down", dve.tensor_tensor(mu[:, :, 5], mu[:, :, 1], mu[:, :, 3], ALU.add))
                mt.wait(dve, "down")

                def lower(i, b):
                    dve.wait_ge(w_hi_s, i + 1)
                    dve.tensor_tensor(w_lo[:, b, :], raw[:, b, :], w_hi[:, b, :].bitcast(F32), ALU.subtract).then_inc(w_lo_s, 1)

                def z_tile(i, b, stored):
                    m = mu[:, bass.ds(i, 1), :].rearrange("p a j -> p (a j)")
                    dve.wait_ge(chunk_free, i * NC + 3 * NC)
                    if stored is not None:
                        dve.wait_ge(z_out[b], stored)
                    adds = []
                    zs, os = z[:, b, 0:TS], zo[:, b, 0:TS]
                    zg, og = (v.rearrange("p (r w) -> p r w", w=GRID_W) for v in (zs, os))
                    zp, op = z[:, b, TS:T], zo[:, b, TS:T]
                    adds = [(og[:, :, 1:], zg[:, :, :-1], 0), (op[:, 1:], zp[:, :-1], 4),
                            (og[:, :, :-1], zg[:, :, 1:], 1), (op[:, :-1], zp[:, 1:], 5),
                            (os[:, GRID_W:], zs[:, :-GRID_W], 2), (os[:, :-GRID_W], zs[:, GRID_W:], 3)]
                    dve.tensor_scalar(zo[:, b, :], z[:, b, :], m[:, 6:7], None, ALU.mult).then_inc(own, 1)
                    for n, (dst, src, j) in enumerate(adds):
                        dve.wait_ge(own, i * ADDS + (n + 1))
                        ins = dve.scalar_tensor_tensor(dst, src, m[:, j:j + 1], dst, ALU.mult, ALU.add)
                        if n < ADDS - 1:
                            ins.then_inc(own, 1)
                        else:
                            ins.then_inc(shifted, 1)
                    dve.wait_ge(shifted, i + 1)
                    dve.sem_inc(z_free, 1)

                norm.dve_head(dve)
                lower(0, 0)
                norm.dve_chunk(dve, 0)
                lower(1, 1)
                norm.dve_chunk(dve, 1)
                norm.dve_chunk(dve, 2)
                for b in range(2):
                    z_tile(b, b, None)
                    lower(b + 2, b)
                with dve.Fori(1, PAIRS) as i:
                    for b in range(2):
                        z_tile(i * 2 + b, b, i * 16)
                        lower(i * 2 + (b + 2), b)
                z_tile(LAST, LAST % 2, 16 * PAIRS)
                for n in range(2 * PAIRS + 2, TILES):
                    lower(n, n % 2)


def fourier_stage(nc, io, sb, u, md, xd):
    H = TS // 2
    HT = H // P
    with Stage(nc) as st, nc.psum_tensor("fo_ps", [P, 8, 512], F32) as ps, \
            nc.sbuf_tensor("fo_f", [P, 2, 256], F32) as feat, nc.sbuf_tensor("fo_eo", [P, 2, NP, H], F32) as eo, \
            nc.sbuf_tensor("fo_t", [P, HT, 2, NP, P], F32) as f, nc.sbuf_tensor("fo_fp", [P, NP, 256], F32) as fp, \
            nc.sbuf_tensor("fo_fh", [1, NP, P], F32) as fh, \
            nc.sbuf_tensor("fo_tab", [P, HT, 2, H], F32) as tab, nc.sbuf_tensor("fo_tabp", [P, 2, TP], F32) as tabp, \
            nc.sbuf_tensor("fo_alt", [P, H], F32) as alt, nc.sbuf_tensor("fo_s", [P, NP, H], F32) as sine, \
            nc.sbuf_tensor("fo_y", [P, NP, T], F32) as y:
        feat_in, tabp_in, alt_in, y_out = st.sem("feat_in"), st.sem("tabp_in"), st.sem("alt_in"), st.sem("y_out")
        tab_in, x_out = st.sem("tab_in"), st.sem("x_out")
        TOK = [f"{a}{t}" for a in "eo" for t in range(HT)]
        pe_t = Steps(st.sem("pe_s"), ["p0", "p1", "h"] + TOK + ["prompt", "mid"] + [f"{n}{j}" for j in range(NP) for n in "SC"])
        dve_t = Steps(st.sem("dve_s"), ["zero", "first", "e", "o"] + [n for n in TOK if n[0] == "e"] + ["mid"] +
                      [f"{n}{j}" for j in range(NP) for n in ("plus", "minus")])
        act_t = Steps(st.sem("act_s"), ["p0", "p1", "h"] + [n for n in TOK if n[0] == "o"] + ["prompt"] +
                      [f"S{j}" for j in range(NP)])
        with st.block() as block:
            @block.sync
            def _(sp):
                sp.dma_start(feat[:, :, :], io["feat"]).then_inc(feat_in, 16)
                sp.dma_start(tabp[:, :, :], io["dft_p"]).then_inc(tabp_in, 16)
                sp.dma_start(alt[:, :], io["alternate"]).then_inc(alt_in, 16)
                sp.dma_start(tab[:, :, :, :], io["dft_s"].rearrange("(t p) a n -> p t a n", p=P)).then_inc(tab_in, 16)
                sp.dma_start(xd.rearrange("k p t -> p k t"), sb["x"][:, :, :]).then_inc(x_out, 16)
                act_t.wait(sp, "prompt")
                dve_t.wait(sp, "mid")
                for j in range(NP):
                    dve_t.wait(sp, f"minus{j}")
                    sp.dma_start(md[j, :, :], y[:, j, :]).then_inc(y_out, 16)
                sp.wait_ge(y_out, 16 * NP)
                sp.wait_ge(x_out, 16)

            @block.tensor
            def _(pe):
                pe.wait_ge(feat_in, 16)
                for half in range(2):
                    for q in range(2):
                        last = pe.matmul(ps[:, half, q * 256:(q + 1) * 256], u[:, half * 2 + q, TS:T], feat[:, 1, :],
                                         start=True, stop=True)
                    pe_t.did(f"p{half}", last)
                for j in range(NP):
                    last = pe.matmul(ps[0:1, 2, j * P:(j + 1) * P], u[:, j, H:H + 1], feat[:, 0, 0:P], start=True, stop=True)
                pe_t.did("h", last)
                for n, name in enumerate(TOK):
                    a, t = n // HT, n % HT
                    bank = (3 + n) % 8
                    if t == 0:
                        dve_t.wait(pe, "eo"[a])
                    if bank < 3:
                        act_t.wait(pe, ("p0", "p1", "h")[bank])
                    for j in range(NP):
                        last = pe.matmul(ps[:, bank, j * P:(j + 1) * P], eo[:, a, j, t * P:(t + 1) * P],
                                         feat[:, 0, a * P:(a + 1) * P], start=True, stop=True)
                    pe_t.did(name, last)
                act_t.wait(pe, "p1")
                pe.wait_ge(tabp_in, 16)
                dve_t.wait(pe, f"e{HT - 1}")
                for j in range(NP):
                    for a in range(2):
                        last = pe.matmul(ps[:, 3, j * TP:(j + 1) * TP], fp[:, j, a * P:(a + 1) * P], tabp[:, a, :],
                                         start=a == 0, stop=a == 1)
                pe_t.did("prompt", last)
                pe.wait_ge(alt_in, 16)
                act_t.wait(pe, "h")
                for j in range(NP):
                    for t in range(HT):
                        pe.matmul(ps[:, 4, j:j + 1], f[:, t, 0, j, :], alt[:, 0:1], start=t == 0, stop=False)
                    last = pe.matmul(ps[:, 4, j:j + 1], fh[:, j, :], alt[0:1, 0:1], start=False, stop=True)
                pe_t.did("mid", last)
                pe.wait_ge(tab_in, 16)
                act_t.wait(pe, f"o{HT - 1}")
                act_t.wait(pe, "prompt")
                dve_t.wait(pe, "mid")
                for j in range(NP):
                    for t in range(HT):
                        last = pe.matmul(ps[:, 4 + j, :], f[:, t, 1, j, :], tab[:, t, 1, :], start=t == 0, stop=t == HT - 1)
                    pe_t.did(f"S{j}", last)
                    for t in range(HT):
                        pe.matmul(ps[:, j, :], f[:, t, 0, j, :], tab[:, t, 0, :], start=t == 0, stop=False)
                    pe_t.did(f"C{j}", pe.matmul(ps[:, j, :], fh[:, j, :], alt[0:1, :], start=False, stop=True))

            @block.vector
            def _(dve):
                dve_t.did("zero", dve.memset(eo[:, 1, :, 0:1], 0.0))
                dve_t.did("first", dve.tensor_copy(eo[:, 0, :, 0:1], u[:, :, 0:1]))
                for a, op in enumerate((ALU.add, ALU.subtract)):
                    dve_t.did("eo"[a], dve.tensor_tensor(eo[:, a, :, 1:H], u[:, :, 1:H], u[:, :, TS - 1:H:-1], op))
                for t in range(HT):
                    pe_t.wait(dve, f"e{t}")
                    dve_t.did(f"e{t}", dve.tensor_copy(f[:, t, 0, :, :],
                                                       ps[:, (3 + t) % 8, :].rearrange("p (j n) -> p j n", j=NP)))
                pe_t.wait(dve, "mid")
                dve_t.did("mid", dve.tensor_copy(y[:, :, H:H + 1], ps[:, 4, 0:NP].unsqueeze(2)))
                for j in range(NP):
                    pe_t.wait(dve, f"C{j}")
                    act_t.wait(dve, f"S{j}")
                    dve_t.did(f"plus{j}", dve.tensor_tensor(y[:, j, 0:H], ps[:, j, :], sine[:, j, :], ALU.add))
                    dve_t.did(f"minus{j}", dve.tensor_tensor(y[:, j, TS - 1:H:-1], ps[:, j, 1:H], sine[:, j, 1:H], ALU.subtract))

            @block.scalar
            def _(act):
                for half in range(2):
                    pe_t.wait(act, f"p{half}")
                    act_t.did(f"p{half}", act.activation(fp[:, half * 2:half * 2 + 2, :],
                                                         ps[:, half, :].rearrange("p (q n) -> p q n", q=2), ACT.Copy))
                pe_t.wait(act, "h")
                act_t.did("h", act.activation(fh[:, :, :], ps[0:1, 2, :].rearrange("p (j n) -> p j n", j=NP), ACT.Copy))
                for t in range(HT):
                    pe_t.wait(act, f"o{t}")
                    act_t.did(f"o{t}", act.activation(f[:, t, 1, :, :],
                                                      ps[:, (3 + HT + t) % 8, :].rearrange("p (j n) -> p j n", j=NP), ACT.Copy))
                pe_t.wait(act, "prompt")
                act_t.did("prompt", act.activation(y[:, :, TS:T], ps[:, 3, :].rearrange("p (j n) -> p j n", j=NP), ACT.Copy))
                for j in range(NP):
                    pe_t.wait(act, f"S{j}")
                    act_t.did(f"S{j}", act.activation(sine[:, j, :], ps[:, 4 + j, :], ACT.Copy))


def output_stage(nc, io, sb, md, xd):
    RAW, MS = 2, 4
    x = sb["x"]
    with Stage(nc) as st, nc.psum_tensor("op_ps", [P, 8, 512], F32) as ps, \
            nc.sbuf_tensor("op_m", [P, MS, T], F32) as m, nc.sbuf_tensor("op_hi", [P, KD, T], F32R) as m_hi, \
            nc.sbuf_tensor("op_lo", [P, KD, T], F32R) as m_lo, nc.sbuf_tensor("op_raw", [P, RAW, D], F32) as raw, \
            nc.sbuf_tensor("op_whi", [P, 2, D], F32R) as w_hi, nc.sbuf_tensor("op_wlo", [P, 2, D], F32R) as w_lo:
        m_in, raw_in = [st.sem(f"m_in{n}") for n in range(MS)], [st.sem(f"raw_in{n}") for n in range(2)]
        x_in = st.sem("x_in")
        act_t = Steps(st.sem("act_s"), ["w0", "w1"] + [f"m{k}" for k in range(KD)] + [f"w{o}" for o in range(2, KD)])
        dve_t = Steps(st.sem("dve_s"), ["w0", "w1"] + [f"m{k}" for k in range(KD)] +
                      [n for o in range(KD) for n in [f"x{o}_{c}" for c in range(NC)] + [f"w{o + 2}"] * (o + 2 < KD)])
        pe_t = Steps(st.sem("pe_s"), [f"o{o}_{c}" for o in range(KD) for c in range(NC)])
        wsrc = io["w_out"][0].rearrange("(k p) n -> p k n", p=P)
        with st.block() as block:
            @block.sync
            def _(sp):
                def load(o):
                    sp.dma_start(raw[:, o % 2, :].rearrange("p (k n) -> p k n", k=KD), wsrc[:, :, o * P:(o + 1) * P])\
                        .then_inc(raw_in[o % 2], 16)
                load(0)
                load(1)
                for k in range(KD):
                    if k >= MS:
                        dve_t.wait(sp, f"m{k - MS}")
                    sp.dma_start(m[:, k % MS, :], md[k, :, :]).then_inc(m_in[k % MS], 16)
                sp.dma_start(x[:, :, :], xd.rearrange("k p t -> p k t")).then_inc(x_in, 16)
                for o in range(2, KD):
                    dve_t.wait(sp, f"w{o - 2}")
                    load(o)

            @block.scalar
            def _(act):
                def upper(o):
                    act.wait_ge(raw_in[o % 2], 16 * (o // 2 + 1))
                    if o >= 2:
                        pe_t.wait(act, f"o{o - 2}_{NC - 1}")
                    act_t.did(f"w{o}", act.activation(w_hi[:, o % 2, :], raw[:, o % 2, :], ACT.Copy))
                upper(0)
                upper(1)
                for k in range(KD):
                    act.wait_ge(m_in[k % MS], 16 * (k // MS + 1))
                    act_t.did(f"m{k}", act.activation(m_hi[:, k, :], m[:, k % MS, :], ACT.Copy))
                for o in range(2, KD):
                    upper(o)

            @block.tensor
            def _(pe):
                def product(o, c, k):
                    ks, cols = slice(k * P, (k + 1) * P), slice(c * CW, (c + 1) * CW)
                    return mm3(pe, ps[:, (o * NC + c) % 8, 0:CW], w_hi[:, o % 2, ks], w_lo[:, o % 2, ks],
                               m_hi[:, k, cols], m_lo[:, k, cols], k == 0, k == KD - 1)
                for k in range(KD):
                    dve_t.wait(pe, f"m{k}")
                    for o in range(2):
                        for c in range(NC):
                            last = product(o, c, k)
                            if k == KD - 1:
                                pe_t.did(f"o{o}_{c}", last)
                for o in range(2, KD):
                    dve_t.wait(pe, f"w{o}")
                    for c in range(NC):
                        n = o * NC + c
                        if n >= 8:
                            dve_t.wait(pe, f"x{(n - 8) // NC}_{(n - 8) % NC}")
                        for k in range(KD):
                            last = product(o, c, k)
                        pe_t.did(f"o{o}_{c}", last)

            @block.vector
            def _(dve):
                def lower(o):
                    act_t.wait(dve, f"w{o}")
                    dve_t.did(f"w{o}", dve.tensor_tensor(w_lo[:, o % 2, :], raw[:, o % 2, :],
                                                         w_hi[:, o % 2, :].bitcast(F32), ALU.subtract))
                lower(0)
                lower(1)
                for k in range(KD):
                    act_t.wait(dve, f"m{k}")
                    dve_t.did(f"m{k}", dve.tensor_tensor(m_lo[:, k, :], m[:, k % MS, :], m_hi[:, k, :].bitcast(F32), ALU.subtract))

                dve.wait_ge(x_in, 16)
                for o in range(KD):
                    for c in range(NC):
                        pe_t.wait(dve, f"o{o}_{c}")
                        for s, a, b in parts(c):
                            xs = x[:, o, c * CW + a:c * CW + b]
                            last = dve.scalar_tensor_tensor(xs, ps[:, (o * NC + c) % 8, a:b],
                                                            sb["mod"][:, 5 * KD + o, s:s + 1], xs, ALU.mult, ALU.add)
                        dve_t.did(f"x{o}_{c}", last)
                    if o + 2 < KD:
                        lower(o + 2)


class Rwkv:

    def __init__(self, nc, ctx):
        def sbuf(name, shape, dt=F32):
            return ctx.enter_context(nc.sbuf_tensor("rw_" + name, shape, dt))
        self.lora = sbuf("lora", [P, 3, T])
        self.reset = sbuf("reset", [P, T], BF16)
        self.w2, self.a2, self.g2 = sbuf("w2", [P, P]), sbuf("a2", [P, P]), sbuf("g2", [P, P])
        self.pp = sbuf("pp", [P, 10])
        self.pn = sbuf("pn", [P, 10])
        self.kk = sbuf("kk", [P, T])
        self.sq = sbuf("sq", [P, T])
        self.bonus = sbuf("bonus", [P, T])
        self.inv = sbuf("inv", [P, 2 * NT])
        self.rkv = sbuf("rkv", [P, 3, T])
        self.ar = sbuf("ar", [P, 2, 2, T])
        self.bk = sbuf("bk", [P, 2, NCH, 2, HS])
        self.gr = sbuf("gr", [P, 2, 2, NCH, 2 * HS])
        self.bt = sbuf("bt", [P, 2, NCH, P])
        self.sv = sbuf("sv", [P, 2, 2, NCH, HS])
        wt = sbuf("wt", [P, 2, 2, NCH, HS])
        self.wt = wt[0:HS]
        self.work = sbuf("work", [P, 6144])
        self.pc = sbuf("pc", [P, 2, NCH])
        self.m = sbuf("m", [P, 2, 2, HS])
        self.mp = sbuf("mp", [P, 2, HS])
        self.m0 = sbuf("m0", [P, 2, HS])
        self.st = sbuf("st", [P, 2, HS])
        w = wt[:, :, :, :, :].rearrange("p d h c n -> p (d h c n)")
        g = self.gr[:, :, :, :, :].rearrange("p d h c n -> p (d h c n)")
        self.sw, self.ai = [[w[:, n * T:(n + 1) * T] for n in (m, m + 1)] for m in (0, 2)]
        self.e1, self.e2 = [[g[:, n * T:(n + 1) * T] for n in (m, m + 1)] for m in (0, 2)]


def by_chunk(t):
    return t.rearrange("p (c n) -> p c n", c=NCH)


def reverse(t, d):
    return t[:, ::-1] if d else t


def head_sums(pe, sb, ps, x):
    for t in range(NT):
        last = pe.matmul(ps[:, 2 * t:2 * t + 2], x[:, t * P:(t + 1) * P], sb["cst"][:, C_BLK:C_BLK + P:HS],
                         start=True, stop=True)
    return last


def spread(pe, sb, ps, wide, c):
    for t in range(NC):
        last = pe.matmul(ps[:, t * P:(t + 1) * P], wide[:, (c * NC + t) * P:(c * NC + t + 1) * P],
                         sb["cst"][:, C_ID:C_ID + P], start=True, stop=True)
    return last


def widen(eng, wide, inv):
    return eng.tensor_copy(wide.rearrange("p (u n) -> p u n", n=HS), inv[:, :].unsqueeze(2).to_broadcast([P, 2 * NT, HS]))


PP = {n: i for i, n in enumerate(("w0_0", "w0_1", "a0_0", "a0_1", "k_k", "k_a", "r_k", "ln_w", "ln_b", "one_ka"))}


class Prep:

    ITEMS = ["ss"] + [f"{n}_{c}" for n in ("a0", "kk", "w0", "a1", "w1") for c in range(NC)]

    def __init__(self, st, io, sb, rw, zd, p, ps):
        self.io, self.sb, self.rw, self.zd, self.p, self.ps = io, sb, rw, zd, p, ps
        self.z_in, self.w_in = [st.sem(f"z_in{n}") for n in range(3)], [st.sem(f"w_in{n}") for n in range(2)]
        self.pe_t = Steps(st.sem("prep_pe"), self.ITEMS)
        self.act_t = Steps(st.sem("prep_act"), ["kraw", "sq"] + [x for i in range(NCH) for x in self.act_names(i)])
        self.dve_t = Steps(st.sem("prep_dve"), ["pn", "ka1"] + [x for i in range(NCH) for x in self.dve_names(i)])

    def items(self, i):
        return self.ITEMS[i - 1:i] if i else []

    def act_names(self, i):
        out = [x for x in self.items(i) if x[0] in "wa"]
        return out + {2: ["sqrt"], 5: ["kda0"], 14: ["kda1"]}.get(i, [])

    def dve_names(self, i):
        out = [x for x in self.items(i) if x[0] not in "wa"]
        return out + {3: ["inv", "wide"], 6: ["kd0"], 9: ["ak0"], 12: ["scan0"], 15: ["kd1"], 16: ["ak1"],
                      17: ["kds", "rkk", "scan1"]}.get(i, [])

    def of(self, name):
        return (self.act_t if name[0] in "wa" else self.dve_t)

    def par(self, name):
        return self.rw.pn[:, PP[name]:PP[name] + 1]

    def sync(self, sp):
        rw, cols = self.rw, bass.ds(self.p * P, P)
        for n in (1, 0, 2):
            sp.dma_start(rw.rkv[:, n, :], self.zd[bass.ds(self.p + NP * n, 1), :, :].rearrange("a p t -> p (a t)"))\
              .then_inc(self.z_in[n], 16)
        for dst, name, sem in ((rw.w2, "decay_w2", self.w_in[0]), (rw.a2, "iclr_a2", self.w_in[1])):
            sp.dma_start(dst[:, :], self.io[name][0].rearrange("d i n -> (d i) n")[:, cols]).then_inc(sem, 16)

    def pe(self, pe, i):
        rw = self.rw
        for name in self.items(i):
            n = self.ITEMS.index(name)
            if n >= 2:
                before = self.ITEMS[n - 2]
                self.of(before).wait(pe, before)
            bank = self.ps[:, n % 2, :]
            if name == "ss":
                self.act_t.wait(pe, "sq")
                last = head_sums(pe, self.sb, bank, rw.sq[:, :])
            else:
                c = int(name[-1])
                if name[0] in "wa":
                    d, which = int(name[1]), "wa".index(name[0])
                    rows = slice(HS * d, HS * d + HS)
                    pe.wait_ge(self.w_in[which], 16)
                    last = pe.matmul(bank[:, 0:CW], (rw.w2, rw.a2)[which][rows, :], rw.lora[rows, which, c * CW:(c + 1) * CW],
                                     start=True, stop=True)
                else:
                    self.dve_t.wait(pe, "wide")
                    last = spread(pe, self.sb, bank, rw.sq[:, :], c)
            self.pe_t.did(name, last)

    def act(self, act, i):
        rw, t = self.rw, self.act_t
        if i == 0:
            act.wait_ge(self.z_in[1], 16)
            self.dve_t.wait(act, "ka1")
            t.did("kraw", act.activation(rw.kk[:, :], rw.rkv[:, 1, :], ACT.Identity, scale=self.par("k_k")))
            t.wait(act, "kraw")
            t.did("sq", act.activation(rw.sq[:, :], rw.kk[:, :], ACT.Square))
        for name in self.act_names(i):
            if name == "sqrt":
                self.dve_t.wait(act, "ss")
                t.did(name, act.activation(rw.inv[:, :], rw.inv[:, :], ACT.Sqrt))
            elif name.startswith("kda"):
                d = int(name[-1])
                t.wait(act, f"a{d}_{NC - 1}")
                t.did(name, act.activation(rw.bk[:, d, :, 1, :], by_chunk(rw.ai[d]), ACT.Identity, bias=self.par("one_ka"),
                                           scale=self.par("k_a")))
            else:
                d, c = int(name[1]), int(name[-1])
                self.pe_t.wait(act, name)
                dst = (rw.sw if name[0] == "w" else rw.ai)[d]
                t.did(name, act.activation(dst[:, c * CW:(c + 1) * CW], self.ps[:, self.ITEMS.index(name) % 2, 0:CW],
                                           ACT.Sigmoid, bias=self.par(f"{name[0]}0_{d}")))

    def dve(self, dve, i):
        rw, t = self.rw, self.dve_t
        if i == 0:
            at = PRM["w0"][0]
            t.did("pn", dve.tensor_copy(
                rw.pn[:, 0:9].unsqueeze(2),
                self.sb["prm"][:, at:at + 36].rearrange("p (n f) -> p n f", f=4)[:, :, bass.ds(self.p, 1)]))
            t.wait(dve, "pn")
            t.did("ka1", dve.tensor_scalar(self.par("one_ka"), self.par("k_a"), -1.0, 1.0, ALU.mult, ALU.add))
        for name in self.dve_names(i):
            d = int(name[-1]) if name[-1].isdigit() else None
            if name == "ss":
                self.pe_t.wait(dve, "ss")
                ins = dve.tensor_scalar(rw.inv[:, :], self.ps[:, 0, 0:2 * NT], 1e-24, None, ALU.max)
            elif name == "inv":
                self.act_t.wait(dve, "sqrt")
                ins = dve.reciprocal(rw.inv[:, :], rw.inv[:, :])
            elif name == "wide":
                t.wait(dve, "inv")
                ins = widen(dve, rw.sq[:, :], rw.inv)
            elif name.startswith("kk_"):
                self.pe_t.wait(dve, name)
                cols = slice(d * CW, (d + 1) * CW)
                ins = dve.tensor_tensor(rw.kk[:, cols], self.ps[:, self.ITEMS.index(name) % 2, 0:CW], rw.kk[:, cols], ALU.mult)
            elif name.startswith("kd") and d is not None:
                self.act_t.wait(dve, f"kda{d}")
                ins = dve.tensor_tensor(rw.bk[:, d, :, 1, :], rw.bk[:, d, :, 1, :], by_chunk(rw.rkv[:, 1, :]), ALU.mult)
            elif name.startswith("ak"):
                t.wait(dve, f"kk_{NC - 1}")
                ins = dve.tensor_tensor(rw.bk[:, d, :, 0, :], by_chunk(rw.ai[d]), by_chunk(rw.kk[:, :]), ALU.mult)
            elif name.startswith("scan"):
                t.wait(dve, f"ak{d}")
                self.act_t.wait(dve, f"w{d}_{NC - 1}")
                ins = dve.tensor_tensor_scan(reverse(rw.ai[d], d), rw.reset[:, :], reverse(rw.sw[d], d), 0.0, ALU.mult, ALU.add)
            elif name == "kds":
                t.wait(dve, "kd1")
                dve.wait_ge(self.z_in[0], 16)
                self.pe_t.wait(dve, f"kk_{NC - 1}")
                ins = dve.tensor_tensor(by_chunk(rw.sq[:, :]), rw.bk[:, 0, :, 1, :], rw.bk[:, 1, :, 1, :], ALU.add)
            else:
                t.wait(dve, "kds")
                ins = dve.scalar_tensor_tensor(rw.sq[:, :], rw.sq[:, :], self.par("r_k"), rw.rkv[:, 0, :], ALU.mult, ALU.mult)
            t.did(name, ins)


def rw_first(nc, io, sb, rw, zd):
    with Stage(nc) as st, nc.psum_tensor(fresh("f_ps"), [P, 2, 512], F32) as ps:
        lora_in, lora_s, ones = st.sem("lora_in"), st.sem("lora_s"), st.sem("ones")
        prep = Prep(st, io, sb, rw, zd, 0, ps)
        with st.block() as block:
            @block.sync
            def _(sp):
                sp.dma_start(rw.lora[:, :, :], zd[NZ - 3:NZ, :, :].rearrange("k p t -> p k t")).then_inc(lora_in, 16)
                prep.sync(sp)
                for sem in prep.z_in + prep.w_in:
                    sp.wait_ge(sem, 16)

            @block.tensor
            def _(pe):
                pe.wait_ge(lora_s, 1)
                for i in range(NCH):
                    prep.pe(pe, i)

            @block.scalar
            def _(act):
                act.wait_ge(lora_in, 16)
                act.activation(rw.lora[:, 0, :], rw.lora[:, 0, :], ACT.Tanh)
                act.activation(rw.lora[:, 2, :], rw.lora[:, 2, :], ACT.Sigmoid).then_inc(lora_s, 1)
                for i in range(NCH):
                    prep.act(act, i)

            @block.vector
            def _(dve):
                dve.memset(rw.reset[:, :], 1.0).then_inc(ones, 1)
                dve.wait_ge(ones, 1)
                dve.memset(rw.reset[:, ::HS], 0.0).then_inc(ones, 1)
                dve.wait_ge(ones, 2)
                for i in range(NCH):
                    prep.dve(dve, i)


def rw_turn(nc, io, sb, rw, md, p, done, more):
    y, yb, wide, c2 = (rw.work[:, n * T:(n + 1) * T] for n in range(4))
    b3 = lambda t: t.rearrange("p (c n) -> p c n", c=NC)
    inv = rw.mp[:, 0, 0:2 * NT]
    par = lambda n: rw.pp[:, PP[n]:PP[n] + 1]
    DONE = ("mean", "var", "rstd", "gate", "y", "centre", "inv", "wide", "norm", "bonus", "sq", "sqrt", "affine")
    part = lambda names: [n for n in names.split() if (done if n in DONE else more)]
    with Stage(nc) as st, nc.psum_tensor(fresh("p_ps"), [P, 8, 512], F32) as ps:
        lo, hi = ps[:, 0:3, 0:CW], ps[:, 3:6, 0:CW]
        pe_t = Steps(st.sem("pe_s"), part("mean gate var rstd rkk"))
        dve_t = Steps(st.sem("dve_s"), part("y pc0 R0 Lp0 centre B0 K0 pc1 R1 Lp1 var B1 inv wide K1 A0 norm A1 bonus gate next pp"))
        act_t = Steps(st.sem("act_s"), part("P0 iP0 sq P1 iP1 Pp0 sqrt Pp1 affine"))
        y_out, s_in, g_in = st.sem("y_out"), st.sem("s_in"), st.sem("g_in")
        with st.block() as block:
            @block.sync
            def _(sp):
                if more:
                    for d, name in enumerate(("state_fwd", "state_bwd")):
                        sp.dma_start(rw.st[:, d, :],
                                     io[name][0, 0, bass.ds((p + 1) * 2, 2), :, :].rearrange("h v k -> (h v) k"))\
                          .then_inc(s_in, 16)
                    if done:
                        pe_t.wait(sp, "gate")
                    sp.dma_start(rw.g2[:, :], io["gate_g2"][0][:, bass.ds((p + 1) * P, P)]).then_inc(g_in, 16)
                if done:
                    dve_t.wait(sp, "gate")
                    sp.dma_start(md[bass.ds(p + NP, 1), :, :].rearrange("a p t -> p (a t)"), y).then_inc(y_out, 16)
                    sp.wait_ge(y_out, 16)
                if more:
                    sp.wait_ge(s_in, 32)
                    sp.wait_ge(g_in, 16)

            @block.tensor
            def _(pe):
                def over(name, out, w, x):
                    for c in range(NC):
                        last = pe.matmul(out[:, c, :], w, x[:, c * CW:(c + 1) * CW], start=True, stop=True)
                    pe_t.did(name, last)
                if done:
                    dve_t.wait(pe, "y")
                    over("mean", lo, sb["cst"][:, C_BLK:C_BLK + P], y)
                    over("gate", hi, rw.g2[:, :], rw.lora[:, 2, :])
                    act_t.wait(pe, "sq")
                    pe_t.did("var", head_sums(pe, sb, ps[:, 6, :], c2))
                    dve_t.wait(pe, "wide")
                    for c in range(NC):
                        last = spread(pe, sb, ps[:, c, :], wide, c)
                    pe_t.did("rstd", last)
                if more:
                    if done:
                        dve_t.wait(pe, "norm")
                    over("rkk", lo, sb["cst"][:, C_BLK:C_BLK + P], rw.sq)

            @block.scalar
            def _(act):
                for name in act_t.names:
                    d = int(name[-1]) if name[-1].isdigit() else None
                    if name == "sq":
                        dve_t.wait(act, "centre")
                        ins = act.activation(c2, y, ACT.Square)
                    elif name == "sqrt":
                        dve_t.wait(act, "var")
                        ins = act.activation(inv, inv, ACT.Sqrt)
                    elif name == "affine":
                        dve_t.wait(act, "norm")
                        ins = act.activation(y, y, ACT.Identity, bias=par("ln_b"), scale=par("ln_w"))
                    elif name.startswith("Pp"):
                        dve_t.wait(act, f"Lp{d}")
                        ins = act.activation(rw.ai[d], rw.ai[d], ACT.Exp, scale=-DECAY)
                    elif name.startswith("iP"):
                        ins = act.activation(rw.e2[d], rw.ai[d], ACT.Exp, scale=DECAY)
                    else:
                        ins = act.activation(rw.e1[d], rw.ai[d], ACT.Exp, scale=-DECAY)
                    act_t.did(name, ins)

            @block.vector
            def _(dve):
                for name in dve_t.names:
                    d = int(name[-1]) if name[-1].isdigit() else None
                    if name == "y":
                        ins = dve.tensor_tensor(y, y, yb, ALU.add)
                    elif name == "centre":
                        pe_t.wait(dve, "mean")
                        ins = dve.scalar_tensor_tensor(b3(y), lo, -1.0 / HS, b3(y), ALU.mult, ALU.add)
                    elif name == "var":
                        pe_t.wait(dve, "var")
                        ins = dve.tensor_scalar(inv, ps[:, 6, 0:2 * NT], 1.0 / HS, GN_EPS, ALU.mult, ALU.add)
                    elif name == "inv":
                        act_t.wait(dve, "sqrt")
                        ins = dve.reciprocal(inv, inv)
                    elif name == "wide":
                        dve_t.wait(dve, "inv")
                        ins = widen(dve, wide, inv)
                    elif name == "norm":
                        pe_t.wait(dve, "rstd")
                        ins = dve.tensor_tensor(b3(y), lo, b3(y), ALU.mult)
                    elif name == "bonus":
                        act_t.wait(dve, "affine")
                        ins = dve.tensor_tensor(y, y, rw.bonus[:, :], ALU.add)
                    elif name == "gate":
                        pe_t.wait(dve, "gate")
                        dve_t.wait(dve, "bonus")
                        ins = dve.tensor_tensor(b3(y), hi, b3(y), ALU.mult)
                    elif name == "next":
                        pe_t.wait(dve, "rkk")
                        if done:
                            dve_t.wait(dve, "bonus")
                        ins = dve.tensor_tensor(b3(rw.bonus[:, :]), lo, b3(rw.rkv[:, 2, :]), ALU.mult)
                    elif name == "pp":
                        if done:
                            act_t.wait(dve, "affine")
                        ins = dve.tensor_copy(rw.pp[:, :], rw.pn[:, :])
                    elif name.startswith("pc"):
                        act_t.wait(dve, f"P{d}")
                        ends = slice(0, None, HS) if d else slice(HS - 1, None, HS)
                        ins = dve.tensor_copy(rw.pc[:, d, :], rw.e1[d][:, ends])
                    elif name[0] == "R":
                        ins = dve.tensor_tensor(rw.ar[:, d, 1, :], rw.rkv[:, 0, :], rw.e1[d], ALU.mult)
                    elif name.startswith("Lp"):
                        act_t.wait(dve, f"iP{d}")
                        ins = dve.tensor_tensor(rw.ai[d], rw.ai[d], rw.sw[d], ALU.subtract)
                    elif name[0] in "BK":
                        n = "BK".index(name[0])
                        ins = dve.tensor_tensor(rw.bk[:, d, :, n, :], rw.bk[:, d, :, n, :], by_chunk(rw.e2[d]), ALU.mult)
                    else:
                        act_t.wait(dve, f"Pp{d}")
                        ins = dve.tensor_tensor(rw.ar[:, d, 0, :], rw.kk[:, :], rw.ai[d], ALU.mult)
                    dve_t.did(name, ins)


def rw_chunks(nc, io, sb, rw, nd, wd):
    B, GC, U = 32, 3, 2 * NCH
    NG, NU, NF = NCH // GC, 6, 12
    jobs = [("g", d, n) for d in range(2) for n in range(2 * NG)]
    jobs += [("b", 0, n) for n in range(NG)] + [("v", 0, n) for n in range(NG)]
    jobs += [("a", 0, n) for n in range(NG)] + [("z", 0, n) for n in range(U // NU)] + [("s", 0, 0)]
    jobs += [("b", 1, n) for n in range(NG)] + [("a", 1, n) for n in range(NG)] + [("z", 1, n) for n in range(U // NU)]
    for d in range(2):
        jobs += [(k, d, n) for k in "fw" for n in range(U // NF)] + [("u", d, n) for n in range(U // NU)]
        jobs += [("y", d, n) for n in range(NCH // NU)]
    name = lambda k, d, n: f"{k}{d}_{n}"
    on_dve = lambda k, d, n: k == "g" or (k in "fwuy" and d == 1 and n % 2 == 1)
    bank = {job: n % 8 for n, job in enumerate(jobs)}
    work = rw.work
    blocks = lambda n: work[0:2 * U, n * B * B:(n + 1) * B * B].rearrange("p (i j) -> p i j", i=B)
    tmp, ni, wi = blocks(0), (blocks(1), blocks(2)), (blocks(3), blocks(4))
    units = lambda t: t[0:HS, 0:U * B].rearrange("p (u t) -> p u t", u=U)
    nt = units(rw.kk)
    nat = (units(rw.rkv[:, 0, :]), units(rw.sq))
    fs = (rw.rkv[:, 1, :], rw.rkv[:, 2, :])
    gu = rw.gr[:, :, :, :, :].rearrange("p d h c n -> p d (h c) n")
    wu = rw.wt.rearrange("p d h c n -> p d (h c) n")
    su = rw.sv[:, :, :, :, :].rearrange("p d h c n -> p d (h c) n")
    at = rw.bk[0:HS, :, :, :, :].rearrange("p d c b n -> p d c (b n)")
    first = lambda d: slice(0, B) if d == 0 else slice(B, HS)
    second = lambda d: slice(B, HS) if d == 0 else slice(0, B)
    ident = sb["cst"][:, C_ID:C_ID + P]
    rkv = rw.rkv[:, :, :].rearrange("p n t -> p (n t)")
    rows_of = lambda d, a, b: [f"{k}{d}_{r}" for r in range(a, b) for k in ("times", "minus")]
    G1 = 2 * NG
    dve_names = [name("g", 0, n) for n in range(G1)]
    for n in range(G1):
        dve_names += rows_of(0, n, n + 1) + [name("g", 1, n)]
    NAT0 = 11
    dve_names += ["nt0", "nt1"] + rows_of(0, G1, B - 1) + rows_of(1, 0, NAT0) + ["nat0_0", "nat0_1"] + rows_of(1, NAT0, B - 1)
    dve_names += ["nat1_0", "nat1_1"] + [name(*job) for job in jobs if job[0] != "g" and on_dve(*job)]
    with Stage(nc) as st, nc.psum_tensor(fresh("g_ps"), [P, 8, 512], F32) as ps:
        pe_t = Steps(st.sem("pe_s"), [name(*job) for job in jobs])
        dve_t = Steps(st.sem("dve_s"), dve_names)
        act_t = Steps(st.sem("act_s"), [name(*job) for job in jobs if not on_dve(*job)])
        pool_t = Steps(st.sem("pool_s"), ["zero", "one", "w0", "w1"])
        n_out, n_in, w_out, w_in = ([st.sem(f"{n}{d}") for d in range(2)] for n in ("n_out", "n_in", "w_out", "w_in"))

        def copied(eng, k, d, n):
            (dve_t if on_dve(k, d, n) else act_t).wait(eng, name(k, d, n))

        with st.block() as block:
            @block.sync
            def _(sp):
                def out_of(d, src):
                    for b in range(2):
                        sp.dma_start(nd[d, :, b].rearrange("u r t -> r u t"), src(slice(B * b, B * b + B))).then_inc(n_out[d], 16)
                    sp.wait_ge(n_out[d], 32)
                    sp.dma_start(ni[d].rearrange("p i j -> p (i j)"), nd[d].rearrange("u b r t -> (u b) (r t)"))\
                      .then_inc(n_in[d], 16)

                def back(d, dst):
                    dve_t.wait(sp, f"minus{d}_{B - 2}")
                    sp.dma_start(wd[d].rearrange("u b r t -> (u b) (r t)"), wi[d].rearrange("p i j -> p (i j)"))\
                      .then_inc(w_out[d], 16)
                    sp.wait_ge(w_out[d], 16)
                    for b in range(2):
                        sp.dma_start(dst(slice(B * b, B * b + B)), wd[d, :, b].rearrange("u r t -> r u t")).then_inc(w_in[d], 16)

                dve_t.wait(sp, name("g", 0, 2 * NG - 1))
                out_of(0, lambda rows: gu[rows, 0, :, rows])
                dve_t.wait(sp, "nt1")
                out_of(1, lambda rows: nt[rows])
                pool_t.wait(sp, "w0")
                back(0, lambda rows: wu[rows, 0, :, rows])
                back(1, lambda rows: nat[1][rows])
                for d in range(2):
                    sp.wait_ge(w_in[d], 32)

            @block.gpsimd
            def _(pool):
                both = work[0:2 * U, 3 * B * B:5 * B * B].rearrange("p (d i) -> p d i", d=2)
                pool_t.did("zero", pool.memset(both, 0.0))
                pool_t.wait(pool, "zero")
                pool_t.did("one", pool.memset(both[:, :, ::B + 1], 1.0))
                for d in range(2):
                    pool_t.did(f"w{d}", pool.memset(rw.wt[:, d, :, :, :], 0.0))

            @block.tensor
            def _(pe):
                for n, (k, d, q) in enumerate(jobs):
                    if n >= 8:
                        copied(pe, *jobs[n - 8])
                    out = ps[:, n % 8, :]
                    if k == "g":
                        g, h = divmod(q, 2)
                        rows = slice(HS * h, HS * h + HS)
                        for j in range(GC):
                            c = g * GC + j
                            last = pe.matmul(out[:, j * P:(j + 1) * P], rw.bk[rows, d, c, :, :].rearrange("p b n -> p (b n)"),
                                             rw.ar[rows, d, :, c * HS:(c + 1) * HS], start=True, stop=True)
                    elif k in "bva":
                        for j in range(GC):
                            c = q * GC + j
                            src = {"b": rw.bk[:, d, c, :, :].rearrange("p b n -> p (b n)"),
                                   "v": rkv[:, 2 * T + (c - 1) * HS:2 * T + (c + 1) * HS],
                                   "a": rw.ar[:, d, 0, c * HS:(c + 1) * HS]}[k]
                            last = pe.transpose(out[0:HS if k == "a" else P, j * P:(j + 1) * P], src, ident)
                    elif k == "s":
                        for h in range(2):
                            rows = slice(HS * h, HS * h + HS)
                            for dd in range(2):
                                last = pe.matmul(out[rows, dd * HS:(dd + 1) * HS], rw.st[rows, dd, :],
                                                 ident[rows, HS * h:HS * h + HS], start=True, stop=True)
                    elif k == "z":
                        if q == 0:
                            copied(pe, "g", d, 2 * NG - 1)
                            copied(pe, "v", 0, NG - 1)
                        for j in range(NU):
                            u = q * NU + j
                            last = pe.matmul(out[0:HS, j * HS:(j + 1) * HS], gu[HS:P, d, u, 0:HS], su[HS:P, d, u, :],
                                             start=True, stop=True)
                    elif k == "f":
                        if q == 0:
                            dve_t.wait(pe, f"nat{d}_1")
                        for j in range(NF):
                            u = q * NF + j
                            last = pe.matmul(out[second(d), j * B:(j + 1) * B], gu[first(d), d, u, second(d)],
                                             nat[d][first(d), u, :], start=True, stop=True)
                    elif k == "w":
                        copied(pe, "f", d, q)
                        for j in range(NF):
                            u = q * NF + j
                            last = pe.matmul(out[first(d), j * B:(j + 1) * B], fs[d][second(d), u * B:(u + 1) * B],
                                             wu[second(d), d, u, second(d)], start=True, stop=True)
                    elif k == "u":
                        copied(pe, "z", d, q)
                        copied(pe, "w", d, q * NU // NF)
                        for j in range(NU):
                            u = q * NU + j
                            last = pe.matmul(out[0:HS, j * HS:(j + 1) * HS], wu[:, d, u, :], su[0:HS, d, u, :],
                                             start=True, stop=True)
                    else:
                        copied(pe, "a", d, NG - 1)
                        for m in (1, 2):
                            copied(pe, "w", d, m)
                        for j in range(NU):
                            c = q * NU + j
                            for h in range(2):
                                last = pe.matmul(out[HS * h:HS * h + HS, j * HS:(j + 1) * HS],
                                                 at[:, d, c, HS * h:HS * h + HS], rw.wt[:, d, h, c, :], start=True, stop=True)
                    pe_t.did(name(k, d, q), last)

            def copy_out(eng, tr, k, d, q, copy, neg):
                pe_t.wait(eng, name(k, d, q))
                out = ps[:, bank[k, d, q], 0:GC * P]
                us = slice(q * NU, (q + 1) * NU)
                if k == "b":
                    last = copy(rw.bt[:, d, q * GC:(q + 1) * GC, :], out.rearrange("p (c n) -> p c n", c=GC))
                elif k == "v":
                    src = out[HS:P].rearrange("p (c h n) -> p h c n", c=GC, h=2)
                    for dd in range(2):
                        for h in range(2):
                            last = copy(rw.sv[HS:P, dd, h, q * GC:(q + 1) * GC, :], src[:, h])
                elif k == "a":
                    last = copy(at[:, d, q * GC:(q + 1) * GC, :], out[0:HS].rearrange("p (c n) -> p c n", c=GC))
                elif k == "s":
                    for h in range(2):
                        rows = slice(HS * h, HS * h + HS)
                        last = copy(rw.m0[rows, :, :], out[rows, 0:P].rearrange("p (d n) -> p d n", d=2))
                elif k == "z":
                    last = copy(su[0:HS, d, us, :], out[0:HS].rearrange("p (u n) -> p u n", u=NU))
                elif k == "f":
                    last = copy(fs[d][second(d), q * NF * B:(q + 1) * NF * B], out[second(d)])
                elif k == "w":
                    last = neg(wu[first(d), d, q * NF:(q + 1) * NF, second(d)],
                               out[first(d)].rearrange("p (u n) -> p u n", u=NF))
                elif k == "u":
                    last = neg(gu[0:HS, d, us, 0:HS], out[0:HS].rearrange("p (u n) -> p u n", u=NU))
                else:
                    last = neg(rw.ar[:, d, 0, q * NU * HS:(q + 1) * NU * HS], out)
                tr.did(name(k, d, q), last)

            @block.vector
            def _(dve):
                def masked(d, q):
                    g, h = divmod(q, 2)
                    pe_t.wait(dve, name("g", d, q))
                    mask = sb["cst"][:, C_MASK + d * P:C_MASK + (d + 1) * P].unsqueeze(1).to_broadcast([P, GC, P])
                    dve_t.did(name("g", d, q), dve.tensor_tensor(
                        rw.gr[:, d, h, g * GC:(g + 1) * GC, :],
                        ps[:, bank["g", d, q], 0:GC * P].rearrange("p (c n) -> p c n", c=GC), mask, ALU.mult))

                def invert(d, a, b):
                    for r in range(a, b):
                        j = B - 1 - r
                        sh = [2 * U, j, B - j]
                        if r == 0:
                            dve.wait_ge(n_in[d], 16)
                            pool_t.wait(dve, "one")
                        if r:
                            dve_t.wait(dve, f"minus{d}_{r - 1}")
                        elif d:
                            dve_t.wait(dve, f"minus0_{B - 2}")
                        t = tmp[:, 0:j, j:B]
                        dve_t.did(f"times{d}_{r}", dve.tensor_tensor(t, ni[d][:, 0:j, j:j + 1].to_broadcast(sh),
                                                                     wi[d][:, j:j + 1, j:B].to_broadcast(sh), ALU.mult))
                        dve_t.wait(dve, f"times{d}_{r}")
                        dve_t.did(f"minus{d}_{r}", dve.tensor_tensor(wi[d][:, 0:j, j:B], wi[d][:, 0:j, j:B], t, ALU.subtract))

                for n in range(G1):
                    masked(0, n)
                for n in range(G1):
                    invert(0, n, n + 1)
                    masked(1, n)
                dve_t.wait(dve, name("g", 1, G1 - 1))
                for b in range(2):
                    rows = slice(B * b, B * b + B)
                    dve_t.did(f"nt{b}", dve.transpose(nt[rows, :, :], gu[rows, 1, :, rows]))
                invert(0, G1, B - 1)
                invert(1, 0, NAT0)
                dve.wait_ge(w_in[0], 32)
                for b in range(2):
                    rows = slice(B * b, B * b + B)
                    dve_t.did(f"nat0_{b}", dve.transpose(nat[0][rows, :, :], wu[rows, 0, :, rows]))
                invert(1, NAT0, B - 1)
                dve.wait_ge(w_in[1], 32)
                pool_t.wait(dve, "w1")
                for b in range(2):
                    rows = slice(B * b, B * b + B)
                    dve_t.did(f"nat1_{b}", dve.transpose(wu[rows, 1, :, rows], nat[1][rows, :, :]))
                for job in jobs:
                    if job[0] != "g" and on_dve(*job):
                        copy_out(dve, dve_t, *job, dve.tensor_copy, lambda o, i: dve.tensor_scalar(o, i, -1.0, None, ALU.mult))

            @block.scalar
            def _(act):
                for job in jobs:
                    if not on_dve(*job):
                        copy_out(act, act_t, *job, lambda o, i: act.activation(o, i, ACT.Copy),
                                 lambda o, i: act.activation(o, i, ACT.Copy, scale=-1.0))


def rw_scan(nc, io, sb, rw, zd, p, more):
    order = [list(range(SCH, NCH)) + list(range(SCH)), list(range(NCH - 1, SCH - 1, -1)) + list(range(SCH - 1, -1, -1))]
    NPC = NCH - SCH
    SD = [(i, d) for i in range(NCH) for d in range(2)]
    y = [rw.work[:, d * T:(d + 1) * T] for d in range(2)]
    with Stage(nc) as st, nc.psum_tensor(fresh("c_ps"), [P, 8, 512], F32) as ps:
        pe_t = Steps(st.sem("pe_s"), [x for i in range(NCH) for x in (f"S{i}_0", f"S{i}_1", f"M{i}_0", f"Y{i}_0", f"M{i}_1", f"Y{i}_1")] +
                     ["st0", "st1"])
        dve_t = Steps(st.sem("dve_s"), ["zero"] + [x for i in range(NCH) for x in
                                                   [f"S{i}_0", f"S{i}_1"] + [f"M{i}_0", f"M{i}_1"]])
        act_t = Steps(st.sem("act_s"), [f"Y{i}_{d}" for i, d in SD] + ["st0", "st1"])
        pool_t = Steps(st.sem("pool_s"), [f"mp{i}_{d}" for i, d in SD])
        out_s = st.sem("out_s")
        prep = Prep(st, io, sb, rw, zd, p + 1, ps[:, 6:8, :]) if more else None
        old = lambda i, d: rw.m0[:, d, :] if i == NPC else rw.m[:, i % 2, d, :]
        with st.block() as block:
            @block.tensor
            def _(pe):
                def s_part(i, d):
                    c = order[d][i]
                    dve_t.wait(pe, f"M{i - 1}_{d}" if i else "zero")
                    if i:
                        act_t.wait(pe, f"Y{i - 1}_{d}")
                    for h in range(2):
                        rows = slice(HS * h, HS * h + HS)
                        last = pe.matmul(ps[0:HS, 2 * d + h, 0:HS], rw.ar[rows, d, 0, c * HS:(c + 1) * HS],
                                         old(i, d)[rows], start=True, stop=True)
                    pe_t.did(f"S{i}_{d}", last)

                def rest(i, d):
                    c = order[d][i]
                    dve_t.wait(pe, f"S{i}_{d}")
                    for h in range(2):
                        rows = slice(HS * h, HS * h + HS)
                        last = pe.matmul(ps[rows, 4 + d, 0:HS], rw.bt[:, d, c, HS * h:HS * h + HS],
                                         rw.sv[:, d, h, c, :], start=True, stop=True)
                    pe_t.did(f"M{i}_{d}", last)
                    for h in range(2):
                        rows = slice(HS * h, HS * h + HS)
                        pe.matmul(ps[rows, 2 * d + h, HS:2 * HS], rw.sv[:, d, h, c, :], rw.gr[:, d, h, c, HS:2 * HS],
                                  start=True, stop=False)
                    for h in range(2):
                        rows = slice(HS * h, HS * h + HS)
                        last = pe.matmul(ps[rows, 2 * d + h, HS:2 * HS], old(i, d)[rows],
                                         rw.ar[rows, d, 1, c * HS:(c + 1) * HS], start=False, stop=True)
                    pe_t.did(f"Y{i}_{d}", last)
                for i, d in SD:
                    s_part(i, d)
                    if d:
                        rest(i, 0)
                        rest(i, 1)
                        if more:
                            prep.pe(pe, i)
                for d in range(2):
                    act_t.wait(pe, f"Y{NCH - 1}_{d}")
                    for h in range(2):
                        rows = slice(HS * h, HS * h + HS)
                        last = pe.matmul(ps[rows, 2 * d + h, HS:2 * HS], rw.st[rows, d, :],
                                         sb["cst"][rows, C_ID + HS * h:C_ID + HS * h + HS], start=True, stop=True)
                    pe_t.did(f"st{d}", last)

            @block.vector
            def _(dve):
                dve_t.did("zero", dve.memset(rw.m[:, 0, :, :], 0.0))
                for i in range(NCH):
                    for d in range(2):
                        c = order[d][i]
                        pe_t.wait(dve, f"S{i}_{d}")
                        dve_t.did(f"S{i}_{d}", dve.tensor_tensor(rw.sv[0:HS, d, :, c, :], ps[0:HS, 2 * d:2 * d + 2, 0:HS],
                                                                 rw.gr[0:HS, d, :, c, 0:HS], ALU.add))
                    for d in range(2):
                        c = order[d][i]
                        new = rw.st[:, d, :] if i == NPC - 1 else rw.m[:, (i + 1) % 2, d, :]
                        pe_t.wait(dve, f"M{i}_{d}")
                        pool_t.wait(dve, f"mp{i}_{d}")
                        dve_t.did(f"M{i}_{d}", dve.scalar_tensor_tensor(new, ps[:, 4 + d, 0:HS], rw.pc[:, d, c:c + 1],
                                                                       rw.mp[:, d, :], ALU.mult, ALU.add))
                    if more:
                        prep.dve(dve, i)

            @block.gpsimd
            def _(pool):
                for i, d in SD:
                    c = order[d][i]
                    if i:
                        dve_t.wait(pool, f"M{i - 1}_{d}")
                    else:
                        dve_t.wait(pool, "zero")
                    pool_t.did(f"mp{i}_{d}", pool.tensor_scalar(rw.mp[:, d, :], old(i, d), rw.pc[:, d, c:c + 1], None, ALU.mult))

            @block.scalar
            def _(act):
                for i, d in SD:
                    c = order[d][i]
                    pe_t.wait(act, f"Y{i}_{d}")
                    for h in range(2):
                        rows = slice(HS * h, HS * h + HS)
                        last = act.activation(y[d][rows, c * HS:(c + 1) * HS], ps[rows, 2 * d + h, HS:2 * HS], ACT.Copy)
                    act_t.did(f"Y{i}_{d}", last)
                    if more and d:
                        prep.act(act, i)
                for d in range(2):
                    pe_t.wait(act, f"st{d}")
                    dve_t.wait(act, f"M{NCH - 1}_{d}")
                    for h in range(2):
                        rows = slice(HS * h, HS * h + HS)
                        last = act.activation(rw.mp[rows, d, :], ps[rows, 2 * d + h, HS:2 * HS], ACT.Copy)
                    act_t.did(f"st{d}", last)

            @block.sync
            def _(sp):
                if more:
                    prep.sync(sp)
                    for sem in prep.z_in + prep.w_in:
                        sp.wait_ge(sem, 16)
                for d, name in enumerate(("state_f", "state_b")):
                    act_t.wait(sp, f"st{d}")
                    sp.dma_start(io[name][0, 0, bass.ds(p * 2, 2), :, :].rearrange("h v k -> (h v) k"), rw.mp[:, d, :])\
                      .then_inc(out_s, 16)
                sp.wait_ge(out_s, 32)


def rwkv(nc, io, sb, zd, md):
    with ExitStack() as ctx:
        rw = Rwkv(nc, ctx)
        nd = nc.dram_tensor("n_dram", [2, 2 * NCH, 2, 32, 32], F32).ap()
        wd = nc.dram_tensor("w_dram", [2, 2 * NCH, 2, 32, 32], F32).ap()
        rw_first(nc, io, sb, rw, zd)
        rw_turn(nc, io, sb, rw, md, -1, False, True)

        def pair(p, more):
            rw_chunks(nc, io, sb, rw, nd, wd)
            rw_scan(nc, io, sb, rw, zd, p, more)
            rw_turn(nc, io, sb, rw, md, p, True, more)

        with nc.Fori(0, NP - 1) as p:
            pair(p, True)
        pair(NP - 1, False)


def mixer(nc, io, sb, zd, md, xd):
    with nc.sbuf_tensor("mx_u", [P, NP, T], F32) as u:
        with nc.sbuf_tensor("h1_hi", [P, KD, T], F32R) as h_hi, nc.sbuf_tensor("h1_lo", [P, KD, T], F32R) as h_lo:
            project_stage(nc, io, sb, h_hi, h_lo, zd, u)
        fourier_stage(nc, io, sb, u, md, xd)


def out_stage(nc, io, sb, y):
    with Stage(nc) as st, nc.psum_tensor("ou_ps", [P, 8, 512], F32) as ps, nc.sbuf_tensor("ou_y", [P, 4, D], F32) as rows, \
            nc.sbuf_tensor("ou_n", [P, 3, T], F32) as tmp, nc.sbuf_tensor("ou_inv", [P, NT], F32) as inv:
        norm = Norm(st, sb, 3, y, None, [tmp[:, n, :] for n in range(3)], inv, ps, 4, (5, 6, 7))
        turned, stored = st.sem("turned"), [st.sem(f"stored{n}") for n in range(4)]
        copied = {0: st.sem("copied_dve"), 1: st.sem("copied_act")}
        with st.block() as block:
            @block.tensor
            def _(pe):
                for n in range(2 * NT):
                    t, half = n // 2, n % 2
                    if n % (2 * NC) == 0:
                        norm.pe(pe, t // NC)
                        norm.ready(pe, t // NC)
                    if n >= 4:
                        pe.wait_ge(copied[n % 2], (n - 4) // 2 + 1)
                    for k in range(4):
                        last = pe.transpose(ps[:, n % 4, k * P:(k + 1) * P], y[:, half * 4 + k, t * P:(t + 1) * P],
                                            sb["cst"][:, C_ID:C_ID + P])
                    last.then_inc(turned, 1)

            def copy(eng, half, c, do):
                for t in range(c * NC, (c + 1) * NC):
                    eng.wait_ge(turned, 2 * t + half + 1)
                    if t >= 4:
                        eng.wait_ge(stored[t % 4], 16 * (t // 4))
                    do(rows[:, t % 4, half * 512:(half + 1) * 512], ps[:, (2 * t + half) % 4, :]).then_inc(copied[half], 1)

            @block.vector
            def _(dve):
                norm.dve_head(dve)
                for c in range(NC):
                    norm.dve_chunk(dve, c)
                    copy(dve, 0, c, dve.tensor_copy)

            @block.scalar
            def _(act):
                norm.act_head(act)
                for c in range(NC):
                    norm.act_chunk(act, c)
                    copy(act, 1, c, lambda o, i: act.activation(o, i, ACT.Copy))

            @block.sync
            def _(sp):
                for t in range(NT):
                    sp.wait_ge(copied[0], t + 1)
                    sp.wait_ge(copied[1], t + 1)
                    dst = io["y_sample"][0, t * P:(t + 1) * P, :] if t * P < TS else io["y_prompt"][0, :, :]
                    sp.dma_start(dst, rows[:, t % 4, :]).then_inc(stored[t % 4], 16)
                for n in range(4):
                    sp.wait_ge(stored[n], 16 * len(range(n, NT, 4)))


def program(nc, io, upto=99):
    with ExitStack() as ctx:
        def keep(name, shape, dt=F32):
            return ctx.enter_context(nc.sbuf_tensor(name, shape, dt))

        sb = {"cst": keep("cst", [P, NCST]), "prm": keep("prm", [P, NPRM]), "mod": keep("mod", [P, NMOD * KD, 2]),
              "bmod": keep("bmod", [P, NMOD * KD])}
        zd = nc.dram_tensor("z_dram", [NZ, P, T], F32).ap()
        md = nc.dram_tensor("mixed_dram", [KD, P, T], F32).ap()
        xd = nc.dram_tensor("x_dram", [KD, P, T], F32).ap()
        with nc.sbuf_tensor("x", [P, KD, T], F32) as x:
            sb["x"] = x
            load_stage(nc, io, sb)
            mod_stage(nc, io, sb)
            with nc.sbuf_tensor("h0_hi", [P, KD, T], F32R) as h_hi, nc.sbuf_tensor("h0_lo", [P, KD, T], F32R) as h_lo:
                ffn_stage(nc, io, sb, 0, h_hi, h_lo)
            mixer(nc, io, sb, zd, md, xd)
        rwkv(nc, io, sb, zd, md)
        with nc.sbuf_tensor("x_again", [P, KD, T], F32) as x:
            sb["x"] = x
            output_stage(nc, io, sb, md, xd)
            if upto >= 3:
                with nc.sbuf_tensor("h2_hi", [P, KD, T], F32R) as h_hi, nc.sbuf_tensor("h2_lo", [P, KD, T], F32R) as h_lo:
                    ffn_stage(nc, io, sb, 1, h_hi, h_lo)
            with nc.sbuf_tensor("y", [P, KD, T], F32) as y:
                out_stage(nc, io, sb, y)


OUTPUTS = (("y_prompt", (1, TP, D)), ("y_sample", (1, TS, D)), ("state_f", (1, 1, 2 * NP, HS, HS)),
           ("state_b", (1, 1, 2 * NP, HS, HS)))


def kernel(**inputs):
    import concourse.bacc as bacc
    from concourse.bass_utils import run_bass_kernel_spmd

    nc = bacc.Bacc("TRN2", target_bir_lowering=False, num_devices=1)
    arrays = {name: np.ascontiguousarray(a) for name, a in inputs.items()}
    for name, a in zip(("consts", "feat", "dft_s", "dft_p", "alternate"), constants()):
        arrays[name] = np.ascontiguousarray(a)
    io = {name: nc.dram_tensor(name, a.shape, mybir.dt.from_np(a.dtype), kind="ExternalInput").ap()
          for name, a in arrays.items()}
    for name, shape in OUTPUTS:
        io[name] = nc.dram_tensor(name, shape, F32, kind="ExternalOutput").ap()
    program(nc, io)
    result = run_bass_kernel_spmd(nc, [arrays], core_ids=[0]).results[0]
    return tuple(result[name] for name, _ in OUTPUTS)
```
